# Optimizing a Trainium2 kernel written in Bass

```python
import jax, jax.numpy as jnp
from jax import lax
import numpy as np

D_MODEL = 2048
BATCH = 1
SEQ = 256
DEPTH = 1

HEAD_DIM = 64
N_Q_HEADS = 32
N_KV_HEADS = 4
GROUP = N_Q_HEADS // N_KV_HEADS
WINDOW = 128
BLOCK = 128
D_ATTN = N_Q_HEADS * HEAD_DIM
D_KV = N_KV_HEADS * HEAD_DIM
D_RNN = 2560
N_RNN_BLOCKS = 16
RNN_BLOCK_W = D_RNN // N_RNN_BLOCKS
RNN_CONV_W = 4
LRU_C = 8.0
D_FF = 3 * D_MODEL
FFN_CONV_W = 3
LN_EPS = 1e-5
ALPHA = (2 * DEPTH) ** 0.25
BETA = (8 * DEPTH) ** -0.25
SPLIT_SIZES = (D_ATTN, D_KV, D_KV, D_RNN, D_RNN, 2 * D_MODEL)
SPLIT_POINTS = tuple(int(s) for s in np.cumsum(SPLIT_SIZES)[:-1])
D_IN = int(sum(SPLIT_SIZES))
V_START = D_ATTN + D_KV

kernel_name = "hybrid_swa_rglru_gated_merge_deepnorm"

def alibi_slopes(n_heads):
    h = np.arange(1, n_heads + 1, dtype=np.float32)
    return jnp.asarray(2.0 ** (-8.0 * h / n_heads), dtype=jnp.float32)

def layer_norm(x, g, b):
    x32 = x.astype(jnp.float32)
    mu = jnp.mean(x32, axis=-1, keepdims=True)
    var = jnp.mean(jnp.square(x32 - mu), axis=-1, keepdims=True)
    y = (x32 - mu) * lax.rsqrt(var + LN_EPS) * g.astype(jnp.float32) + b.astype(jnp.float32)
    return y.astype(x.dtype)

def causal_dwconv(x, w, b):
    width = w.shape[0]
    s = x.shape[1]
    xp = jnp.pad(x, ((0, 0), (width - 1, 0), (0, 0)))
    y = sum(xp[:, k:k + s] * w[k] for k in range(width))
    return y + b

def sliding_window_attention(q, k, v, sinks):
    bsz, s = q.shape[0], q.shape[1]
    nb = s // BLOCK
    qb = q.reshape(bsz, nb, BLOCK, N_KV_HEADS, GROUP, HEAD_DIM)

    def band(t):
        tb = t.reshape(bsz, nb, BLOCK, N_KV_HEADS, HEAD_DIM)
        prev = jnp.pad(tb, ((0, 0), (1, 0), (0, 0), (0, 0), (0, 0)))[:, :-1]
        return jnp.concatenate([prev, tb], axis=2)

    kb, vb = band(k), band(v)
    scores = jnp.einsum('bnqhgd,bnkhd->bhgnqk', qb, kb).astype(jnp.float32) * (HEAD_DIM ** -0.5)
    qi = jnp.arange(BLOCK)[:, None]
    kj = jnp.arange(2 * BLOCK)[None, :]
    dist = BLOCK + qi - kj
    blk = jnp.arange(nb)[:, None, None]
    key_pos = (blk - 1) * BLOCK + kj
    valid = (dist >= 0) & (dist < WINDOW) & (key_pos >= 0)
    slopes = alibi_slopes(N_Q_HEADS).reshape(N_KV_HEADS, GROUP, 1, 1, 1)
    scores = scores - slopes * dist.astype(jnp.float32)
    scores = jnp.where(valid, scores, -jnp.inf)
    sink = sinks.astype(jnp.float32).reshape(N_KV_HEADS, GROUP, 1, 1, 1)
    m = jnp.maximum(jnp.max(scores, axis=-1, keepdims=True), sink)
    p = jnp.exp(scores - m)
    denom = jnp.sum(p, axis=-1, keepdims=True) + jnp.exp(sink - m)
    p = (p / denom).astype(v.dtype)
    o = jnp.einsum('bhgnqk,bnkhd->bnqhgd', p, vb)
    return o.reshape(bsz, s, D_ATTN)

def rg_lru(x, w_a, b_a, w_i, b_i, lam):
    bsz, s, _ = x.shape
    xb = x.reshape(bsz, s, N_RNN_BLOCKS, RNN_BLOCK_W)
    r = jax.nn.sigmoid(jnp.einsum('bsnc,ncd->bsnd', xb, w_a).reshape(bsz, s, D_RNN) + b_a)
    i = jax.nn.sigmoid(jnp.einsum('bsnc,ncd->bsnd', xb, w_i).reshape(bsz, s, D_RNN) + b_i)
    log_a = -LRU_C * r.astype(jnp.float32) * jax.nn.softplus(-lam.astype(jnp.float32))
    a = jnp.exp(log_a)
    u = jnp.sqrt(-jnp.expm1(2.0 * log_a)) * (i * x).astype(jnp.float32)

    def combine(left, right):
        a_l, b_l = left
        a_r, b_r = right
        return a_l * a_r, a_r * b_l + b_r

    _, h = lax.associative_scan(combine, (a, u), axis=1)
    return h.astype(x.dtype)

def setup_inputs(seed: int = 0) -> dict:
    key = jax.random.key(seed)
    ks = jax.random.split(key, 24)
    f32 = jnp.float32
    L = DEPTH
    nrm = lambda k, shape, scale: jax.random.normal(k, shape, f32) * scale
    x = jax.random.normal(ks[0], (BATCH, SEQ, D_MODEL), f32)
    w_in = nrm(ks[1], (L, D_MODEL, D_IN), D_MODEL ** -0.5)
    w_in = w_in.at[:, :, V_START:V_START + D_KV].multiply(BETA)
    b_gate = nrm(ks[2], (L, 2 * D_MODEL), 0.1)
    rnn_conv_w = nrm(ks[3], (L, RNN_CONV_W, D_RNN), RNN_CONV_W ** -0.5)
    rnn_conv_b = nrm(ks[4], (L, D_RNN), 0.02)
    lru_wa = nrm(ks[5], (L, N_RNN_BLOCKS, RNN_BLOCK_W, RNN_BLOCK_W), RNN_BLOCK_W ** -0.5)
    lru_ba = nrm(ks[6], (L, D_RNN), 0.02)
    lru_wi = nrm(ks[7], (L, N_RNN_BLOCKS, RNN_BLOCK_W, RNN_BLOCK_W), RNN_BLOCK_W ** -0.5)
    lru_bi = nrm(ks[8], (L, D_RNN), 0.02)
    a_c = jax.random.uniform(ks[9], (L, D_RNN), f32, minval=0.9, maxval=0.999)
    a0 = a_c ** (1.0 / LRU_C)
    lru_lambda = jnp.log(a0) - jnp.log1p(-a0)
    attn_sinks = nrm(ks[10], (L, N_Q_HEADS), 0.5)
    w_attn_proj = nrm(ks[11], (L, D_ATTN, D_MODEL), BETA * D_ATTN ** -0.5)
    w_rnn_proj = nrm(ks[12], (L, D_RNN, D_MODEL), BETA * D_RNN ** -0.5)
    w_out = nrm(ks[13], (L, D_MODEL, D_MODEL), BETA * D_MODEL ** -0.5)
    ln1_g = 1.0 + nrm(ks[14], (L, D_MODEL), 0.02)
    ln1_b = nrm(ks[15], (L, D_MODEL), 0.02)
    ffn_w_up = nrm(ks[16], (L, D_MODEL, D_FF), D_MODEL ** -0.5)
    ffn_w_gate = nrm(ks[17], (L, D_MODEL, D_FF), D_MODEL ** -0.5)
    ffn_conv_w = nrm(ks[18], (L, FFN_CONV_W, D_FF), FFN_CONV_W ** -0.5)
    ffn_conv_b = nrm(ks[19], (L, D_FF), 0.02)
    ffn_w_down = nrm(ks[20], (L, D_FF, D_MODEL), BETA * D_FF ** -0.5)
    ln2_g = 1.0 + nrm(ks[21], (L, D_MODEL), 0.02)
    ln2_b = nrm(ks[22], (L, D_MODEL), 0.02)
    return {"x": x, "w_in": w_in, "b_gate": b_gate, "rnn_conv_w": rnn_conv_w,
            "rnn_conv_b": rnn_conv_b, "lru_wa": lru_wa, "lru_ba": lru_ba, "lru_wi": lru_wi,
            "lru_bi": lru_bi, "lru_lambda": lru_lambda, "attn_sinks": attn_sinks,
            "w_attn_proj": w_attn_proj, "w_rnn_proj": w_rnn_proj, "w_out": w_out,
            "ln1_g": ln1_g, "ln1_b": ln1_b, "ffn_w_up": ffn_w_up, "ffn_w_gate": ffn_w_gate,
            "ffn_conv_w": ffn_conv_w, "ffn_conv_b": ffn_conv_b, "ffn_w_down": ffn_w_down,
            "ln2_g": ln2_g, "ln2_b": ln2_b}

def reference(x, w_in, b_gate, rnn_conv_w, rnn_conv_b, lru_wa, lru_ba, lru_wi, lru_bi,
              lru_lambda, attn_sinks, w_attn_proj, w_rnn_proj, w_out, ln1_g, ln1_b,
              ffn_w_up, ffn_w_gate, ffn_conv_w, ffn_conv_b, ffn_w_down, ln2_g, ln2_b):
    bsz, s, _ = x.shape
    for l in range(DEPTH):
        proj = x @ w_in[l]
        q, k, v, rx, ry, gl = jnp.split(proj, SPLIT_POINTS, axis=-1)
        q = q.reshape(bsz, s, N_Q_HEADS, HEAD_DIM)
        k = k.reshape(bsz, s, N_KV_HEADS, HEAD_DIM)
        v = v.reshape(bsz, s, N_KV_HEADS, HEAD_DIM)
        y_attn = sliding_window_attention(q, k, v, attn_sinks[l]) @ w_attn_proj[l]
        rx = causal_dwconv(rx, rnn_conv_w[l], rnn_conv_b[l])
        hr = rg_lru(rx, lru_wa[l], lru_ba[l], lru_wi[l], lru_bi[l], lru_lambda[l])
        y_rnn = (hr * jax.nn.gelu(ry, approximate=True)) @ w_rnn_proj[l]
        g_attn, g_rnn = jnp.split(jax.nn.sigmoid(gl + b_gate[l]), 2, axis=-1)
        mix = (g_attn * y_attn + g_rnn * y_rnn) @ w_out[l]
        x = layer_norm(ALPHA * x + mix, ln1_g[l], ln1_b[l])
        up = x @ ffn_w_up[l]
        gate = causal_dwconv(x @ ffn_w_gate[l], ffn_conv_w[l], ffn_conv_b[l])
        f = (jax.nn.gelu(gate, approximate=True) * up) @ ffn_w_down[l]
        x = layer_norm(ALPHA * x + f, ln2_g[l], ln2_b[l])
    return x


_drawn_inputs = setup_inputs


def setup_inputs(seed=0):
    import zlib

    import numpy as np

    out = dict(_drawn_inputs(seed))
    spreads = {}
    factors = {'b_gate': 51.72,
     'rnn_conv_b': 53.4,
     'lru_wa': 29.688,
     'lru_ba': 64.0,
     'lru_bi': 64.0,
     'lru_lambda': 27.528,
     'attn_sinks': 28.187,
     'ffn_conv_b': 8.0,
     'ln2_g': 7.645,
     'ln2_b': 7.817,
     'rnn_conv_w': 8.0,
     'lru_wi': 8.0,
     'w_rnn_proj': 8.0}
    for name, (base, spread) in spreads.items():
        noise = np.random.default_rng([zlib.crc32(name.encode()), seed]).standard_normal(out[name].shape)
        drawn = base * np.exp(spread * noise) if base else spread * noise
        out[name] = __import__('jax').numpy.asarray(drawn.astype(out[name].dtype))
    for name, factor in factors.items():
        out[name] = (out[name] * factor).astype(out[name].dtype)
    return out
```

```python
from contextlib import ExitStack

import concourse.bass as bass
from concourse import mybir

F32 = mybir.dt.float32
F32R = mybir.dt.float32r
ACT = mybir.ActivationFunctionType
ALU = mybir.AluOpType
AX = mybir.AxisListType

P = 128
T = 256
TOK = T // P
D = 2048
KT = D // P
HD = 64
NH, NKV = 32, 4
D_KV = NKV * HD
D_RNN = 2560
RT = D_RNN // P
RB = 160
GRP = 5
D_FF = 3 * D
FT_HALF = D_FF // P // 2
LN_EPS = 1e-5
ALPHA = 2.0 ** 0.25
LRU_C = 8.0
SCALE = HD ** -0.5

COL_Q, COL_KV, COL_RX = 0, D, D + 2 * D_KV
COL_RY = COL_RX + D_RNN
COL_GA = COL_RY + D_RNN
COL_GR = COL_GA + D

PANELS = {}
_n = 0
for _name, _count in (("rx", 4), ("ry", 4), ("rnn", 4), ("q", 4), ("kv", 1), ("gr", 4), ("ga", 4),
                      ("attn", 4), ("out", 4), ("ff0", 12), ("down0", 4), ("ff1", 12), ("down1", 4)):
    PANELS[_name] = _n
    _n += _count
UNITS = {}
_u = 0
for _name, _count in (("rx", 32), ("ry", 32), ("rnn", 32), ("q", 32), ("kv", 8), ("gr", 32), ("ga", 32),
                      ("attn", 32), ("out", 32), ("ff0", 96), ("down0", 48), ("ff1", 96), ("down1", 48)):
    UNITS[_name] = _u
    _u += _count
LAST_UNIT = _u

WIDE = 1280
SLIM = 1024

LRU_LO = [0, 0, 1, 2, 3]
LRU_HI = [1, 2, 3, 4, 4]
LRU_AT = [0, 2, 5, 8, 11]
LRU_TILES = 13
LRU_PIECES = []
for _b in range(4):
    for _t in range(GRP):
        _r0, _r1 = max(RB * _b, P * _t), min(RB * _b + RB, P * _t + P)
        if _r0 < _r1:
            LRU_PIECES.append((_b, _r0 - RB * _b, _r1 - _r0, _t))

PAR_BG, PAR_CW, PAR_CB, PAR_BA, PAR_BI, PAR_LAM = 0, 32, 112, 132, 152, 172
PAR_FW, PAR_FB = 192, 336
PAR_COLS = 384

CONST_ID, CONST_SLOPE, CONST_COLS = 0, P, P + NH


def layer_kernel(nc, consts, x, w_in, b_gate, rnn_conv_w, rnn_conv_b, lru_wa, lru_ba, lru_wi, lru_bi,
                 lru_lambda, attn_sinks, w_attn_proj, w_rnn_proj, w_out, ln1_g, ln1_b, ffn_w_up,
                 ffn_w_gate, ffn_conv_w, ffn_conv_b, ffn_w_down, ln2_g, ln2_b, out):
    ds = bass.ds

    with ExitStack() as ctx:
        BASE = (nc.sbuf_base + 63) // 64 * 64

        def at(name, offset, shape, dt=F32):
            return nc.alloc_sbuf_tensor_at(name, shape, dt, offset=BASE + offset)

        def sem(name):
            return ctx.enter_context(nc.semaphore(name))

        raw = at("raw", 0, [P, 4, 2 * WIDE])
        w_hi = at("w_hi", 40960, [P, 4, WIDE], F32R)
        w_lo = at("w_lo", 61440, [P, 4, WIDE], F32R)
        raw_tail = at("raw_tail", 0, [P, 4, 2 * WIDE])[:, :, 2 * SLIM:]
        gate_sig = at("gate_sig", 40960, [P, 4, WIDE])[:, :, SLIM:]
        q_now = at("q_now", 61440, [P, 4, WIDE])[:, :, SLIM:]
        k_now = raw_tail[:, 0, 0:T]
        v_now = raw_tail[:, 0, T:T + TOK * HD].rearrange("p (b d) -> p b d", b=TOK)
        probs_t = [raw_tail[:, 1, 0:3 * P], raw_tail[:, 2, 0:3 * P]]
        act_t = at("act_t", 81920, [P, KT, 2, T], F32R)
        SMALL = 81920 + 32768
        const = at("const", SMALL, [P, CONST_COLS])
        par = at("par", SMALL + 640, [P, PAR_COLS])
        sinks = at("sinks", SMALL + 2176, [P, NH])
        coef = at("coef", SMALL + 2304, [P, 9, RT])
        smax = at("smax", SMALL + 3040, [P, 4, 3])
        ssmall = at("ssmall", SMALL + 3104, [P, 6, 8])
        stats = at("stats", SMALL + 3296, [P, TOK, 4, 6])
        lnv = at("lnv", SMALL + 3488, [P, TOK, 6])
        ident = const[:, CONST_ID:CONST_ID + P]
        dist = raw_tail[:, 3, 0:3 * P]
        BIG = SMALL + 3584
        x_tok = at("x_tok", BIG + 20480, [P, TOK, D])
        par_rows = at("par_rows", BIG + 20480 + 16384, [P, 4, P])
        xc = at("xc", BIG, [P, RT, T])
        g_t = at("g_t", BIG + 20480, [P, RT, 2, T], F32R)
        lru_w = at("lru_w", BIG + 61440, [P, 2, LRU_TILES * P])
        lru_r = at("lru_r", BIG + 74752, [P, GRP, T])
        lru_i = at("lru_i", BIG + 79872, [P, GRP, T])
        lru_a = at("lru_a", BIG + 84992, [P, GRP, T])
        g_work = at("g_work", BIG + 20480, [P, RT, 2, T])
        merge = at("merge", BIG, [P, KT, T])
        g_attn = at("g_attn", BIG + 16384, [P, KT, T])
        q_all = at("q_all", BIG + 32768, [P, KT, T])
        k_dup = at("k_dup", BIG + 49152, [P, NKV, T])
        v_all = at("v_all", BIG + 53248, [P, TOK, D_KV])
        o_t = at("o_t", BIG + 55296, [P, KT, 2, T], F32R)
        s_buf = at("s_buf", BIG + 88064, [P, 4, 3 * P])
        mix_raw = at("mix_raw", BIG + 88064, [P, 4, T])
        res = at("res", BIG, [P, TOK, D])
        ln_gb = at("ln_gb", BIG + 16384, [P, 2, D])
        f_t = at("f_t", BIG + 32768, [P, FT_HALF, 2, T], F32R)
        gate_c = at("gate_c", BIG + 81920, [P, 4, T])
        f_raw = at("f_raw", BIG + 86016, [P, 4, T])
        assert BASE + BIG + 88064 + 6144 <= nc.sbuf_usable_end

        bank = [ctx.enter_context(nc.psum_tensor(f"bank{b}", [P, 512], F32)) for b in range(8)]
        ACC = [[bank[0], bank[1], bank[2]], [bank[3], bank[4], bank[5]]]
        gate_bank = [bank[6], bank[7]]
        s_bank = [bank[6], bank[7]]
        pt_bank = [bank[2], bank[6]]
        o_bank = [bank[5], bank[7]]

        dist_loaded = sem("dist_loaded")
        const_loaded, x_loaded, par_loaded = sem("const_loaded"), [sem("x0_loaded"), sem("x1_loaded")], sem("par_loaded")
        lru_zeroed, lru_w_loaded = sem("lru_zeroed"), sem("lru_w_loaded")
        par_turned, par_made, coef_step, coef_exp = sem("par_turned"), sem("par_made"), sem("coef_step"), sem("coef_exp")
        x_turned, x_hi_made, x_lo_made = sem("x_turned"), sem("x_hi_made"), sem("x_lo_made")
        raw_loaded = [sem(f"raw_loaded{s}") for s in range(4)]
        hi_made, lo_made, unit_used = sem("hi_made"), sem("lo_made"), sem("unit_used")
        acc_free = sem("acc_free")
        conv_step = sem("conv_step")
        gates_done, gates_read = sem("gates_done"), sem("gates_read")
        a_made, th_made, v_made, root_made = sem("a_made"), sem("th_made"), sem("v_made"), sem("root_made")
        lru_step, h_made = sem("lru_step"), sem("h_made")
        g_prod, g_hi, g_lo = sem("g_prod"), sem("g_hi"), sem("g_lo")
        staged = sem("staged")
        scores_done, scores_taken = sem("scores_done"), sem("scores_taken")
        soft_step, bias_made, exp_made, probs_made = sem("soft_step"), sem("bias_made"), sem("exp_made"), sem("probs_made")
        pt_done, pt_taken, pv_done, o_hi, o_lo = sem("pt_done"), sem("pt_taken"), sem("pv_done"), sem("o_hi"), sem("o_lo")
        merged = sem("merged")
        attn_gated, mix_sum, mix_hi, mix_lo = sem("attn_gated"), sem("mix_sum"), sem("mix_hi"), sem("mix_lo")
        res_loaded, ln_loaded = sem("res_loaded"), sem("ln_loaded")
        res_step, stat_step, ln_step, ln_root = sem("res_step"), sem("stat_step"), sem("ln_step"), sem("ln_root")
        ln_turned, ln_hi, ln_lo = sem("ln_turned"), sem("ln_hi"), sem("ln_lo")
        ff_conv, ff_gelu, ff_prod, ff_hi, ff_lo = sem("ff_conv"), sem("ff_gelu"), sem("ff_prod"), sem("ff_hi"), sem("ff_lo")
        out_stored, act_waited = sem("out_stored"), sem("act_waited")

        def load_chunk(sp, w_rows, chunk, kc, width, col, rot, slot, first=False):
            if not first:
                sp.wait_ge(lo_made, rot * 8 + 2 * slot - 6)
            src = w_rows.rearrange("(k p) n -> p k n", p=P)[:, kc * chunk:kc * chunk + kc, ds(col, width)]
            sp.dma_start(raw[:, slot, 0:kc * width].rearrange("p (k n) -> p k n", k=kc), src)\
              .then_inc(raw_loaded[slot], 16)

        def load_panels(sp, w_rows, n, rot, count, kc, width, col):
            for pp in range(count):
                for c in range(4):
                    load_chunk(sp, w_rows, c, kc, width, (n + pp) * width + col, rot + pp, c)

        def split_hi(act, unit, j, size, refill=True):
            slot, chunk = j % 4, j // 2 % 4
            if j % 2 == 0:
                act.wait_ge(raw_loaded[chunk], (unit + j // 8 * 8) * 2 + 16)
            if refill:
                act.wait_ge(unit_used, unit + j - 3)
            half = j % 2 * size
            nc.scalar.activation(w_hi[:, slot, 0:size], raw[:, chunk, half:half + size], ACT.Copy)\
                .then_inc(hi_made, 1)

        def split_lo(dve, unit, j, size):
            slot, chunk, half = j % 4, j // 2 % 4, j % 2 * size
            dve.wait_ge(hi_made, unit + j + 1)
            nc.vector.tensor_tensor(w_lo[:, slot, 0:size], raw[:, chunk, half:half + size],
                                    w_hi[:, slot, 0:size].bitcast(F32), ALU.subtract).then_inc(lo_made, 1)

        PASSES = ((w_hi, 0), (w_hi, 1), (w_lo, 0))

        def panel_features(pe, unit, j0, acc, moving, kc, width, between=lambda j: None, columns=None):
            size = kc * width // 2
            tiles = width // P if columns is None else columns // P
            for j in range(8):
                slot = (j0 + j) % 4
                pe.wait_ge(lo_made, unit + j0 + j + 1)
                last = None
                for c in range(tiles):
                    dst = acc[c // 2][:, c % 2 * T:c % 2 * T + T]
                    for k in range(kc):
                        at_ = k * width + c * P
                        if at_ // size != j % 2:
                            continue
                        kt = j // 2 * kc + k
                        for n, (w, part) in enumerate(PASSES):
                            last = nc.tensor.matmul(dst, w[:, slot, at_ % size:at_ % size + P], moving[:, kt, part, :],
                                                    start=(kt == 0 and n == 0 and c % 2 == 0),
                                                    stop=(j == 7 and n == 2 and kt == 4 * kc - 1), skip_group_check=True)
                if columns is not None:
                    for t in range(TOK):
                        for k in range(kc):
                            at_ = k * width + columns
                            if at_ // size != j % 2:
                                continue
                            kt = j // 2 * kc + k
                            for n, (w, part) in enumerate(((w_hi, 0), (w_lo, 0), (w_hi, 1))):
                                last = nc.tensor.matmul(acc[1][:, t * T:t * T + T], moving[:, kt, part, t * P:t * P + P],
                                                        w[:, slot, at_ % size:at_ % size + width - columns],
                                                        start=(kt == 0 and n == 0 and t == 0),
                                                        stop=(j == 7 and n == 2 and kt == 4 * kc - 1), skip_group_check=True)
                last.then_inc(unit_used, 1)
                between(j)

        def panel_tokens(pe, unit, j0, acc, stationary, chunks):
            for j in range(2 * chunks):
                slot = (j0 + j) % 4
                pe.wait_ge(lo_made, unit + j0 + j + 1)
                for t in range(TOK):
                    for k in range(2):
                        kt = 2 * j + k
                        for n, (w, part) in enumerate(((w_hi, 0), (w_lo, 0), (w_hi, 1))):
                            last = nc.tensor.matmul(acc[t][:, :], stationary[:, kt, part, t * P:t * P + P],
                                                    w[:, slot, k * 512:k * 512 + 512],
                                                    start=(kt == 0 and n == 0),
                                                    stop=(kt == 4 * chunks - 1 and n == 2))
                last.then_inc(unit_used, 1)

        def acc_of(name, pp):
            return ACC[(PANELS[name] + pp) % 2]

        block = ctx.enter_context(nc.Block())

        @block.sync
        def _(sp):
            sp.dma_start(const[:, :], consts[:, 0:CONST_COLS]).then_inc(const_loaded, 16)
            for t in range(TOK):
                sp.dma_start(x_tok[:, t, :], x[0, t * P:t * P + P, :]).then_inc(x_loaded[t], 16)
            rows = {"bg": b_gate[0].rearrange("(t p) -> t p", p=P),
                    "cw": rnn_conv_w[0].rearrange("k (t p) -> (k t) p", p=P),
                    "fw": ffn_conv_w[0].rearrange("k (t p) -> (k t) p", p=P),
                    "fb": ffn_conv_b[0].rearrange("(t p) -> t p", p=P)}
            load_chunk(sp, w_in[0], 0, 4, 640, COL_RX, 0, 0, first=True)
            sp.dma_start(par_rows[0:32, 0, :], rows["bg"]).then_inc(par_loaded, 16)
            sp.dma_start(par_rows[32:112, 0, :], rows["cw"]).then_inc(par_loaded, 16)
            for n, v in enumerate((rnn_conv_b, lru_ba, lru_bi, lru_lambda)):
                sp.dma_start(par_rows[RT * n:RT * n + RT, 1, :], v[0].rearrange("(t p) -> t p", p=P)).then_inc(par_loaded, 16)
            sp.dma_start(par_rows[0:96, 2, :], rows["fw"][0:96]).then_inc(par_loaded, 16)
            sp.dma_start(par_rows[0:48, 3, :], rows["fw"][96:144]).then_inc(par_loaded, 16)
            sp.dma_start(par_rows[48:96, 3, :], rows["fb"]).then_inc(par_loaded, 16)
            sp.dma_start(sinks[:, :], attn_sinks[0].partition_broadcast(P)).then_inc(par_loaded, 16)
            for c in range(1, 4):
                load_chunk(sp, w_in[0], c, 4, 640, COL_RX, 0, c, first=True)

            def load_lru(g):
                for m, w in enumerate((lru_wa, lru_wi)):
                    for b, r0, n, t in LRU_PIECES:
                        row = RB * b + r0 - P * t
                        col = LRU_AT[t] * P + RB * b - LRU_LO[t] * P
                        sp.dma_start(lru_w[row:row + n, m, col:col + RB], w[0, ds(g * 4 + b, 1), r0:r0 + n, :]
                                     .rearrange("a r c -> (a r) c")).then_inc(lru_w_loaded, 16)

            sp.wait_ge(lru_zeroed, 1)
            load_lru(0)
            with sp.Fori(1, 4) as n:
                load_panels(sp, w_in[0], n, n, 1, 4, 640, COL_RX)
            load_panels(sp, w_in[0], 0, 4, 1, 4, 640, COL_RY)
            with sp.Fori(1, 4) as n:
                sp.wait_ge(gates_done, n * GRP)
                load_lru(n)
                load_panels(sp, w_in[0], n, n + 4, 1, 4, 640, COL_RY)
            with sp.Fori(0, 4) as n:
                load_panels(sp, w_rnn_proj[0], n, n + PANELS["rnn"], 1, 5, 512, 0)
            with sp.Fori(0, 5) as n:
                load_panels(sp, w_in[0], n, n + PANELS["q"], 1, 4, 512, COL_Q)
            sp.wait_ge(lo_made, UNITS["rnn"] + 32)
            sp.dma_start(dist, consts[:, CONST_COLS:CONST_COLS + 3 * P]).then_inc(dist_loaded, 16)
            with sp.Fori(0, 4) as n:
                load_panels(sp, w_in[0], n, n + PANELS["gr"], 1, 4, 512, COL_GR)
            with sp.Fori(0, 4) as n:
                load_panels(sp, w_in[0], n, n + PANELS["ga"], 1, 4, 512, COL_GA)
            with sp.Fori(0, 4) as n:
                load_panels(sp, w_attn_proj[0], n, n + PANELS["attn"], 1, 4, 512, 0)
            load_panels(sp, w_out[0], 0, PANELS["out"], 1, 4, 512, 0)
            sp.wait_ge(mix_sum, 4)
            for t in range(TOK):
                sp.dma_start(res[:, t, :], x[0, t * P:t * P + P, :]).then_inc(res_loaded, 16)
            for n, v in enumerate((ln1_g, ln1_b)):
                sp.dma_start(ln_gb[:, n, :], v[0].partition_broadcast(P)).then_inc(ln_loaded, 16)
            with sp.Fori(1, 4) as n:
                load_panels(sp, w_out[0], n, n + PANELS["out"], 1, 4, 512, 0)
            rot = UNITS["ff0"] // 8
            for half in range(2):
                with sp.Fori(0, 6) as n:
                    col = n * 512 + half * 6 * 512
                    load_panels(sp, ffn_w_gate[0], 0, n * 2 + rot, 1, 4, 512, col)
                    load_panels(sp, ffn_w_up[0], 0, n * 2 + rot + 1, 1, 4, 512, col)
                if half == 0:
                    sp.wait_ge(ln_step, LN_STEPS)
                    for n, v in enumerate((ln2_g, ln2_b)):
                        sp.dma_start(ln_gb[:, n, :], v[0].partition_broadcast(P)).then_inc(ln_loaded, 16)
                rot += 12
                w_down = ffn_w_down[0][half * D_FF // 2:(half + 1) * D_FF // 2, :]
                with sp.Fori(0, 2) as n:
                    for c in range(12):
                        load_chunk(sp, w_down, c % 6, 4, 512, n * 1024 + c // 6 * 512, n * 3 + rot + c // 4, c % 4)
                rot += 6
            for t in range(TOK):
                sp.wait_ge(ln_step, LN_STEPS + LN_DONE[t])
                sp.dma_start(out[0, t * P:t * P + P, :], res[:, t, :]).then_inc(out_stored, 16)
            sp.wait_ge(out_stored, 16 * TOK)

        @block.gpsimd
        def _(pool):
            nc.gpsimd.memset(lru_w[:, :, :], 0.0).then_inc(lru_zeroed, 1)
            for g in range(NKV):
                if g == 0:
                    pool.wait_ge(acc_free, PANELS["kv"] + 3)
                else:
                    pool.wait_ge(pv_done, 8 * g)
                nc.gpsimd.tensor_copy(q_now, q_all[:, 4 * g:4 * g + 4, :]).then_inc(staged, 1)
                nc.gpsimd.tensor_copy(k_now, k_dup[:, g, :]).then_inc(staged, 1)
                nc.gpsimd.tensor_copy(v_now, v_all[:, :, HD * g:HD * g + HD]).then_inc(staged, 1)

        @block.tensor
        def _(pe):
            pe.wait_ge(const_loaded, 16)
            pe.wait_ge(x_loaded[0], 16)
            for t in range(TOK):
                if t:
                    pe.wait_ge(x_loaded[t], 16)
                for kt in range(KT):
                    turned = nc.tensor.transpose(bank[kt // 2][:, kt % 2 * T + t * P:kt % 2 * T + t * P + P],
                                                 x_tok[:, t, kt * P:kt * P + P], ident)
                    if t == TOK - 1 and kt % 2:
                        turned.then_inc(x_turned, 1)
            pe.wait_ge(par_loaded, 160)
            pe.wait_ge(x_lo_made, 8)
            col = 0
            for n, rows_ in enumerate((112, 80, 96, 96)):
                turned = nc.tensor.transpose(bank[7][:, col:col + rows_], par_rows[0:rows_, n, :], ident[0:rows_, 0:rows_])
                col += rows_
            turned.then_inc(par_turned, 1)

            with pe.Fori(0, 2) as i:
                for pp in range(2):
                    pe.wait_ge(acc_free, i * 2 + (pp + 1))
                    panel_features(pe, i * 16, 8 * pp, acc_of("rx", pp), act_t, 4, 640)

            pe.wait_ge(conv_step, CONV_STEPS)
            pe.wait_ge(acc_free, PANELS["ry"] + 2)
            with pe.Fori(0, 2) as i:
                for pp in range(2):
                    g = i * 2 + pp
                    pe.wait_ge(lru_w_loaded, (i * 2 + pp + 1) * 256)
                    for c in range(GRP):
                        pe.wait_ge(gates_read, i * 10 + (5 * pp + c + 1))
                        dst = gate_bank[(5 * pp + c) % 2]
                        feeds = [t for t in range(GRP) if LRU_LO[t] <= c <= LRU_HI[t]]
                        for m in range(2):
                            for t in feeds:
                                tile = (LRU_AT[t] + c - LRU_LO[t]) * P
                                done = nc.tensor.matmul(dst[:, m * T:m * T + T], lru_w[:, m, tile:tile + P],
                                                        xc[:, ds(i * 10 + 5 * pp + t, 1), :].rearrange("p a t -> p (a t)"),
                                                        start=(t == feeds[0]), stop=(t == feeds[-1]))
                        done.then_inc(gates_done, 1)
                    pe.wait_ge(acc_free, i * 2 + (PANELS["ry"] + pp + 1))
                    panel_features(pe, i * 16 + UNITS["ry"], 8 * pp, acc_of("ry", pp), act_t, 4, 640)

            pe.wait_ge(g_lo, 5)
            with pe.Fori(0, 2) as i:
                for pp in range(2):
                    pe.wait_ge(acc_free, i * 2 + (PANELS["rnn"] + pp + 1))
                    panel_features(pe, i * 16 + UNITS["rnn"], 8 * pp, acc_of("rnn", pp), g_t, 5, 512)
            with pe.Fori(0, 2) as i:
                for pp in range(2):
                    pe.wait_ge(acc_free, i * 2 + (PANELS["q"] + pp + 1))
                    panel_features(pe, i * 16 + UNITS["q"], 8 * pp, acc_of("q", pp), act_t, 4, 512)
            pe.wait_ge(acc_free, PANELS["kv"] + 1)
            panel_features(pe, UNITS["kv"], 0, acc_of("kv", 0), act_t, 4, 512, columns=D_KV)

            def attention(i, first_head, pp):
                def scores(hh):
                    half = hh % 2 * HD
                    tile = 2 * pp + hh // 2
                    q = q_now[half:half + HD, tile, :]
                    k = k_now[half:half + HD, :]
                    pe.wait_ge(scores_taken, i * 8 + (first_head + 4 * pp + hh + 1))
                    nc.tensor.matmul(s_bank[hh % 2][:, 0:T], q[:, P:T], k, start=True, stop=True)
                    nc.tensor.matmul(s_bank[hh % 2][:, T:3 * P], q[:, 0:P], k[:, 0:P], start=True, stop=True)\
                        .then_inc(scores_done, 1)

                def turn(hh):
                    pe.wait_ge(probs_made, i * 8 + (first_head + 4 * pp + hh + 1))
                    pe.wait_ge(pt_taken, i * 8 + (first_head + 4 * pp + hh + 1))
                    for n, seg in enumerate((2, 0, 1)):
                        turned = nc.tensor.transpose(pt_bank[hh % 2][:, n * P:n * P + P],
                                                     s_buf[:, hh, seg * P:seg * P + P], ident)
                    turned.then_inc(pt_done, 1)

                def values(hh):
                    half = hh % 2 * HD
                    pair = hh // 2
                    if hh % 2 == 0:
                        pe.wait_ge(o_lo, i * 4 + (first_head // 2 + 2 * pp + hh // 2 + 1))
                    pe.wait_ge(pt_taken, i * 8 + (first_head + 4 * pp + hh + 3))
                    nc.tensor.matmul(o_bank[pair][half:half + HD, 0:T], v_now[:, 0, :], probs_t[hh % 2][:, 0:T],
                                     start=True, stop=False, skip_group_check=True)
                    nc.tensor.matmul(o_bank[pair][half:half + HD, P:T], v_now[:, 1, :], probs_t[hh % 2][:, T:3 * P],
                                     start=False, stop=True, skip_group_check=True).then_inc(pv_done, 1)

                def between(j):
                    if j == 0:
                        pe.wait_ge(o_lo, i * 4 + (first_head // 2 + 2 * pp + 2))
                        for hh in range(4):
                            scores(hh)
                    if j == 4:
                        turn(0)
                    if j == 5:
                        turn(1)
                        values(0)
                    if j == 6:
                        turn(2)
                        values(1)
                        turn(3)
                    if j == 7:
                        values(2)
                        values(3)
                return between

            for name, first_head in (("gr", 0), ("ga", 16)):
                with pe.Fori(0, 2) as i:
                    pe.wait_ge(staged, i * 3 + (3 * first_head // 8 + 3))
                    for pp in range(2):
                        pe.wait_ge(acc_free, i * 2 + (PANELS[name] + pp + 1))
                        panel_features(pe, i * 16 + UNITS[name], 8 * pp, acc_of(name, pp), act_t, 4, 512,
                                       between=attention(i, first_head, pp))

            pe.wait_ge(o_lo, NH // 2 + 2)
            with pe.Fori(0, 2) as i:
                for pp in range(2):
                    pe.wait_ge(acc_free, i * 2 + (PANELS["attn"] + pp + 1))
                    panel_features(pe, i * 16 + UNITS["attn"], 8 * pp, acc_of("attn", pp), o_t, 4, 512)

            pe.wait_ge(mix_lo, 4)
            with pe.Fori(0, 2) as i:
                for pp in range(2):
                    pe.wait_ge(acc_free, i * 2 + (PANELS["out"] + pp + 1))
                    panel_tokens(pe, i * 16 + UNITS["out"], 8 * pp, acc_of("out", pp), act_t, 4)

            for t in range(TOK):
                pe.wait_ge(ln_step, LN_DONE[t])
                for kt in range(KT):
                    turned = nc.tensor.transpose(bank[kt // 2][:, kt % 2 * T + t * P:kt % 2 * T + t * P + P],
                                                 res[:, t, kt * P:kt * P + P], ident)
                    if t == TOK - 1 and kt % 2:
                        turned.then_inc(ln_turned, 1)
            pe.wait_ge(ln_lo, 8)
            for half in range(2):
                with pe.Fori(0, 6) as i:
                    for pp in range(2):
                        pe.wait_ge(acc_free, i * 2 + (PANELS[f"ff{half}"] + pp + 1))
                        panel_features(pe, i * 16 + UNITS[f"ff{half}"], 8 * pp, acc_of(f"ff{half}", pp), act_t, 4, 512)
                pe.wait_ge(ff_lo, 6 * (half + 1))
                with pe.Fori(0, 2) as i:
                    for pp in range(2):
                        pe.wait_ge(acc_free, i * 2 + (PANELS[f"down{half}"] + pp + 1))
                        panel_tokens(pe, i * 24 + UNITS[f"down{half}"], 12 * pp, acc_of(f"down{half}", pp), f_t, 6)

        @block.scalar
        def _(act):
            def wait_apart(semaphore, value):
                act.wait_ge(semaphore, value)
                act.sem_inc(act_waited, 1)

            act.sem_inc(gates_read, 2)
            act.sem_inc(pt_taken, 2)
            for kt in range(0, KT, 2):
                act.wait_ge(x_turned, kt // 2 + 1)
                nc.scalar.activation(act_t[:, kt:kt + 2, 0, :], bank[kt // 2][:, :].rearrange("p (k t) -> p k t", k=2),
                                     ACT.Copy).then_inc(x_hi_made, 1)
            for j in range(4):
                split_hi(act, 0, j, WIDE, refill=False)
            act.wait_ge(coef_step, 2)
            nc.scalar.activation(coef[:, 2, :], coef[:, 1, :], ACT.Exp, scale=-1.0).then_inc(coef_exp, 1)

            def refill(i, stride, base, js, size):
                for j in js:
                    split_hi(act, i * stride + base, j + 4, size)

            with act.Fori(0, 2) as i:
                refill(i, 16, 0, range(16), WIDE)

            def lru_v(i, pp):
                return g_work[:, ds(i * 10 + 5 * pp, GRP), 0, :]

            def param(col, i, stride, off):
                return par[:, ds(i * stride + (col + off), 1)]

            with act.Fori(0, 2) as i:
                for pp in range(2):
                    act.wait_ge(g_lo, i * 2 + pp + 1)
                    for c in range(GRP):
                        wait_apart(gates_done, i * 10 + (5 * pp + c + 1))
                        src = gate_bank[(5 * pp + c) % 2]
                        nc.scalar.activation(lru_r[:, c, :], src[:, 0:T], ACT.Sigmoid, bias=param(PAR_BA, i, 10, 5 * pp + c))
                        nc.scalar.activation(lru_i[:, c, :], src[:, T:2 * T], ACT.Sigmoid, bias=param(PAR_BI, i, 10, 5 * pp + c))\
                            .then_inc(gates_read, 1)
                    wait_apart(gates_read, i * 10 + (5 * pp + GRP + 2))
                    for c in range(GRP):
                        nc.scalar.activation(lru_a[:, c, :], lru_r[:, c, :], ACT.Exp,
                                             scale=coef[:, 8, ds(i * 10 + (5 * pp + c), 1)]).then_inc(a_made, 1)
                    for c in range(GRP):
                        nc.scalar.activation(lru_r[:, c, :], lru_r[:, c, :], ACT.Tanh,
                                             scale=coef[:, 7, ds(i * 10 + (5 * pp + c), 1)]).then_inc(th_made, 1)
                    refill(i, 16, UNITS["ry"] + 0, range(8 * pp, 8 * pp + 2), WIDE)
                    act.wait_ge(v_made, i * 2 + (pp + 1))
                    nc.scalar.activation(lru_v(i, pp), lru_v(i, pp), ACT.Sqrt, scale=2.0 ** 64).then_inc(root_made, 1)
                    refill(i, 16, UNITS["ry"] + 0, range(8 * pp + 2, 8 * pp + 8), WIDE)
                    act.wait_ge(unit_used, i * 16 + (UNITS["ry"] + 8 * pp + 8))
                    acc = acc_of("ry", pp)
                    for c in range(GRP):
                        done = nc.scalar.activation(lru_r[:, c, :], acc[c // 2][:, c % 2 * T:c % 2 * T + T], ACT.Gelu_apprx_tanh)
                    done.then_inc(acc_free, 1)
                    wait_apart(g_prod, i * 2 + (pp + 1))
                    nc.scalar.activation(g_t[:, ds(i * 10 + 5 * pp, GRP), 0, :], lru_r[:, :, :], ACT.Copy).then_inc(g_hi, 1)

            def copy_panel(i, name, pp, dst):
                wait_apart(unit_used, i * 16 + (UNITS[name] + 8 * pp + 8))
                for b in range(2):
                    done = nc.scalar.activation(dst[:, ds(i * 8 + (4 * pp + 2 * b), 2), :],
                                                acc_of(name, pp)[b][:, :].rearrange("p (k t) -> p k t", k=2), ACT.Copy)
                done.then_inc(acc_free, 1)

            with act.Fori(0, 1) as i:
                for pp in range(2):
                    refill(i, 16, UNITS["rnn"], range(8 * pp, 8 * pp + 8), WIDE)
                    copy_panel(i, "rnn", pp, merge)
            for pp in range(2, 4):
                refill(0, 16, UNITS["rnn"], range(8 * pp, 8 * pp + 4), WIDE)
                refill(0, 16, UNITS["rnn"], range(8 * pp + 4, 8 * pp + 8), WIDE if pp < 3 else SLIM)
                copy_panel(0, "rnn", pp, merge)
            with act.Fori(0, 2) as i:
                for pp in range(2):
                    refill(i, 16, UNITS["q"], range(8 * pp, 8 * pp + 8), SLIM)
                    copy_panel(i, "q", pp, q_all)
            refill(0, 0, UNITS["kv"], range(8), SLIM)
            act.wait_ge(unit_used, UNITS["kv"] + 8)
            acc = acc_of("kv", 0)
            for parity in range(2):
                for half in range(2):
                    nc.scalar.activation(k_dup[HD * half:HD * half + HD, parity::2, :],
                                         acc[0][HD * parity:HD * parity + HD, :].rearrange("p (k t) -> p k t", k=2), ACT.Copy)
            nc.scalar.activation(v_all[:, :, :], acc[1][:, :].rearrange("p (b d) -> p b d", b=TOK), ACT.Copy)\
                .then_inc(acc_free, 1)

            bias = ssmall[:, 0, :]
            sums = ssmall[:, 2, :]
            for name, first_head, col in (("gr", 0, PAR_BG + KT), ("ga", 16, PAR_BG)):
                with act.Fori(0, 2) as i:
                    for pp in range(2):
                        base = UNITS[name]
                        refill(i, 16, base, range(8 * pp, 8 * pp + 2), SLIM)
                        act.wait_ge(bias_made, i * 2 + (first_head // 4 + pp + 1))
                        for hh in range(4):
                            for blk, (c0, c1) in enumerate(((0, T), (T, 3 * P))):
                                nc.scalar.activation(s_buf[:, hh, c0:c1], s_buf[:, hh, c0:c1], ACT.Exp, scale=SCALE,
                                                     bias=bias[:, 2 * hh + blk:2 * hh + blk + 1],
                                                     accum_out=sums[:, 2 * hh + blk:2 * hh + blk + 1])
                        nc.scalar.activation(ssmall[:, 1, :], ssmall[:, 1, :], ACT.Exp).then_inc(exp_made, 1)

                        def take_pt(hh):
                            act.wait_ge(pt_done, i * 8 + (first_head + 4 * pp + hh + 1))
                            nc.scalar.activation(probs_t[hh % 2], pt_bank[hh % 2][:, 0:3 * P], ACT.Copy).then_inc(pt_taken, 1)

                        def take_o(pair):
                            wait_apart(pv_done, i * 8 + (first_head + 4 * pp + 2 * pair + 2))
                            nc.scalar.activation(o_t[:, ds(i * 4 + (first_head // 2 + 2 * pp + pair), 1), 0, :]
                                                 .rearrange("p a t -> p (a t)"),
                                                 o_bank[pair][:, 0:T], ACT.Copy).then_inc(o_hi, 1)

                        refill(i, 16, base, range(8 * pp + 2, 8 * pp + 5), SLIM)
                        take_pt(0)
                        refill(i, 16, base, range(8 * pp + 5, 8 * pp + 6), SLIM)
                        take_pt(1)
                        refill(i, 16, base, range(8 * pp + 6, 8 * pp + 7), SLIM)
                        act.wait_ge(pv_done, i * 8 + (first_head + 4 * pp + 1))
                        take_pt(2)
                        act.wait_ge(pv_done, i * 8 + (first_head + 4 * pp + 2))
                        take_pt(3)
                        take_o(0)
                        refill(i, 16, base, range(8 * pp + 7, 8 * pp + 8), SLIM)
                        take_o(1)
                        wait_apart(unit_used, i * 16 + (base + 8 * pp + 8))
                        for c in range(4):
                            dst = gate_sig[:, c, :] if name == "gr" else \
                                g_attn[:, ds(i * 8 + (4 * pp + c), 1), :].rearrange("p a t -> p (a t)")
                            done = nc.scalar.activation(dst, acc_of(name, pp)[c // 2][:, c % 2 * T:c % 2 * T + T], ACT.Sigmoid,
                                                        bias=param(col, i, 8, 4 * pp + c))
                        done.then_inc(acc_free, 1)

            with act.Fori(0, 2) as i:
                for pp in range(2):
                    refill(i, 16, UNITS["attn"], range(8 * pp, 8 * pp + 8), SLIM)
                    wait_apart(mix_sum, i * 2 + (pp + 1))
                    nc.scalar.activation(act_t[:, ds(i * 8 + 4 * pp, 4), 0, :], mix_raw[:, :, :], ACT.Copy).then_inc(mix_hi, 1)
            with act.Fori(0, 2) as i:
                refill(i, 16, UNITS["out"], range(16), SLIM)

            def ln_roots(count):
                for t in range(TOK):
                    act.wait_ge(ln_step, LN_VAR[t] + count)
                    nc.scalar.activation(lnv[:, t, 2:3], lnv[:, t, 1:2], ACT.Sqrt).then_inc(ln_root, 1)

            ln_roots(0)
            for kt in range(0, KT, 2):
                act.wait_ge(ln_turned, kt // 2 + 1)
                nc.scalar.activation(act_t[:, kt:kt + 2, 0, :], bank[kt // 2][:, :].rearrange("p (k t) -> p k t", k=2),
                                     ACT.Copy).then_inc(ln_hi, 1)
            for half in range(2):
                with act.Fori(0, 6) as i:
                    base = UNITS[f"ff{half}"]
                    refill(i, 16, base, range(8), SLIM)
                    refill(i, 16, base, range(8, 12), SLIM)
                    act.wait_ge(acc_free, i * 2 + (PANELS[f"ff{half}"] + 3))
                    nc.scalar.activation(gate_c[:, :, :], gate_c[:, :, :], ACT.Gelu_apprx_tanh).then_inc(ff_gelu, 1)
                    refill(i, 16, base, range(12, 16), SLIM)
                    wait_apart(acc_free, i * 2 + (PANELS[f"ff{half}"] + 4))
                    nc.scalar.activation(f_t[:, ds(i * 4, 4), 0, :], f_raw[:, :, :], ACT.Copy).then_inc(ff_hi, 1)
                if half == 0:
                    with act.Fori(0, 2) as i:
                        refill(i, 24, UNITS["down0"], range(24), SLIM)
                else:
                    refill(0, 0, UNITS["down1"], range(44), SLIM)
            ln_roots(LN_STEPS)

        @block.vector
        def _(dve):
            dve.sem_inc(acc_free, 2)
            dve.sem_inc(g_lo, 1)
            dve.sem_inc(scores_taken, 2)
            dve.sem_inc(o_lo, 2)
            for kt in range(0, KT, 2):
                dve.wait_ge(x_hi_made, kt // 2 + 1)
                nc.vector.tensor_tensor(act_t[:, kt:kt + 2, 1, :], bank[kt // 2][:, :].rearrange("p (k t) -> p k t", k=2),
                                        act_t[:, kt:kt + 2, 0, :].bitcast(F32), ALU.subtract).then_inc(x_lo_made, 1)
            for j in range(4):
                split_lo(dve, 0, j, WIDE)
            dve.wait_ge(par_turned, 1)
            nc.vector.tensor_copy(par[:, :], bank[7][:, 0:PAR_COLS]).then_inc(par_made, 1)
            dve.wait_ge(par_made, 1)

            steps = [0]

            def step(ins):
                ins.then_inc(coef_step, 1)
                steps[0] += 1
                dve.wait_ge(coef_step, steps[0])

            lam = par[:, PAR_LAM:PAR_LAM + RT]
            neg, mag, e, s, s2, poly, low = (coef[:, n, :] for n in range(7))
            step(nc.vector.tensor_scalar(neg, lam, -1.0, None, ALU.mult))
            step(nc.vector.tensor_tensor(mag, neg, lam, ALU.max))
            step(nc.vector.tensor_scalar(low, neg, 0.0, None, ALU.max))
            dve.wait_ge(coef_exp, 1)
            step(nc.vector.tensor_scalar(s2, e, 2.0, None, ALU.add))
            step(nc.vector.reciprocal(s2, s2))
            step(nc.vector.tensor_tensor(s, e, s2, ALU.mult))
            step(nc.vector.tensor_tensor(s2, s, s, ALU.mult))
            step(nc.vector.tensor_scalar(poly, s2, 1.0 / 17, None, ALU.mult))
            for n in (15, 13, 11, 9, 7, 5, 3):
                step(nc.vector.scalar_tensor_tensor(poly, poly, 1.0 / n, s2, ALU.add, ALU.mult))
            step(nc.vector.scalar_tensor_tensor(poly, poly, 1.0, s, ALU.add, ALU.mult))
            step(nc.vector.scalar_tensor_tensor(poly, poly, 2.0, low, ALU.mult, ALU.add))
            step(nc.vector.tensor_scalar(coef[:, 7, :], poly, LRU_C, None, ALU.mult))
            step(nc.vector.tensor_scalar(coef[:, 8, :], poly, -LRU_C, None, ALU.mult))

            def refill(i, stride, base, js, size):
                for j in js:
                    split_lo(dve, i * stride + base, j + 4, size)

            def lru_v(i, pp):
                return g_work[:, ds(i * 10 + 5 * pp, GRP), 0, :]

            def column(i, stride, col):
                return par[:, ds(i * stride + col, 1)]

            with dve.Fori(0, 2) as i:
                for pp in range(2):
                    refill(i, 16, 0, range(8 * pp, 8 * pp + 8), WIDE)
                    dve.wait_ge(unit_used, i * 16 + (8 * pp + 8))
                    acc = acc_of("rx", pp)
                    for k in range(4):
                        if k:
                            dve.wait_ge(conv_step, i * 38 + (19 * pp + 5 * k))
                        for c in range(GRP):
                            src = acc[c // 2][:, c % 2 * T:c % 2 * T + T - k]
                            dst = xc[:, ds(i * 10 + (5 * pp + c), 1), k:T].rearrange("p a t -> p (a t)")
                            tap = column(i, 10, PAR_CW + RT * (3 - k) + 5 * pp + c)
                            if k == 0:
                                done = nc.vector.tensor_scalar(dst, src, tap, column(i, 10, PAR_CB + 5 * pp + c), ALU.mult, ALU.add)
                            else:
                                done = nc.vector.scalar_tensor_tensor(dst, src, tap, dst, ALU.mult, ALU.add)
                            done.then_inc(acc_free if k == 3 and c == GRP - 1 else conv_step, 1)

            with dve.Fori(0, 2) as i:
                for pp in range(2):
                    group = xc[:, ds(i * 10 + 5 * pp, GRP), :]
                    dve.wait_ge(gates_read, i * 10 + (5 * pp + GRP + 2))
                    nc.vector.tensor_tensor(lru_i[:, :, :], lru_i[:, :, :], group, ALU.mult).then_inc(lru_step, 1)
                    dve.wait_ge(a_made, i * 10 + (5 * pp + GRP))
                    nc.vector.tensor_tensor(lru_v(i, pp), lru_a[:, :, :], lru_a[:, :, :], ALU.mult).then_inc(lru_step, 1)
                    dve.wait_ge(th_made, i * 10 + (5 * pp + GRP))
                    dve.wait_ge(lru_step, i * 6 + (3 * pp + 2))
                    nc.vector.scalar_tensor_tensor(lru_v(i, pp), lru_v(i, pp), 1.0, lru_r[:, :, :], ALU.add, ALU.mult)\
                        .then_inc(v_made, 1)
                    refill(i, 16, UNITS["ry"], range(8 * pp, 8 * pp + 2), WIDE)
                    dve.wait_ge(root_made, i * 2 + (pp + 1))
                    nc.vector.scalar_tensor_tensor(lru_i[:, :, :], lru_v(i, pp), 2.0 ** -32, lru_i[:, :, :], ALU.mult, ALU.mult)\
                        .then_inc(lru_step, 1)
                    dve.wait_ge(lru_step, i * 6 + (3 * pp + 3))
                    for c in range(GRP):
                        nc.vector.tensor_tensor_scan(xc[:, ds(i * 10 + (5 * pp + c), 1), :].rearrange("p a t -> p (a t)"),
                                                     lru_a[:, c, :], lru_i[:, c, :], 0.0, ALU.mult, ALU.add).then_inc(h_made, 1)
                    refill(i, 16, UNITS["ry"], range(8 * pp + 2, 8 * pp + 8), WIDE)
                    dve.wait_ge(acc_free, i * 2 + (PANELS["ry"] + pp + 3))
                    dve.wait_ge(h_made, i * 10 + (5 * pp + GRP))
                    nc.vector.tensor_tensor(lru_r[:, :, :], lru_r[:, :, :], group, ALU.mult).then_inc(g_prod, 1)
                    dve.wait_ge(g_hi, i * 2 + (pp + 1))
                    nc.vector.tensor_tensor(g_t[:, ds(i * 10 + 5 * pp, GRP), 1, :], lru_r[:, :, :],
                                            g_t[:, ds(i * 10 + 5 * pp, GRP), 0, :].bitcast(F32), ALU.subtract).then_inc(g_lo, 1)

            refill(0, 0, UNITS["rnn"], range(28), WIDE)
            refill(0, 0, UNITS["rnn"], range(28, 32), SLIM)
            with dve.Fori(0, 2) as i:
                refill(i, 16, UNITS["q"], range(16), SLIM)
            refill(0, 0, UNITS["kv"], range(8), SLIM)

            bias, sink_part, sums = ssmall[:, 0, :], ssmall[:, 1, :], ssmall[:, 2, :]
            denom, top = ssmall[:, 3, :], ssmall[:, 4, :]

            def by_block(tile, blk):
                return tile.rearrange("p (h b) -> p h b", b=2)[:, :, blk]

            dve.wait_ge(dist_loaded, 16)
            SOFT = 7
            for name, first_head in (("gr", 0), ("ga", 16)):
                with dve.Fori(0, 2) as i:
                    for pp in range(2):
                        base = UNITS[name]

                        def soft(n):
                            dve.wait_ge(soft_step, i * (2 * SOFT) + (SOFT * (first_head // 4 + pp) + n))

                        sink = sinks[:, ds(i * 8 + (first_head + 4 * pp), 4)]
                        refill(i, 16, base, range(8 * pp, 8 * pp + 1), SLIM)
                        for hh in range(4):
                            dve.wait_ge(scores_done, i * 8 + (first_head + 4 * pp + hh + 1))
                            nc.vector.scalar_tensor_tensor(
                                s_buf[:, hh, :], dist, const[:, ds(i * 8 + (CONST_SLOPE + first_head + 4 * pp + hh), 1)],
                                s_bank[hh % 2][:, 0:3 * P], ALU.mult, ALU.add).then_inc(scores_taken, 1)
                        dve.wait_ge(scores_taken, i * 8 + (first_head + 4 * pp + 4 + 2))
                        nc.vector.tensor_reduce(smax[:, :, :], s_buf[:, :, :].rearrange("p h (s k) -> p h s k", s=3), AX.X, ALU.max)\
                            .then_inc(soft_step, 1)
                        soft(1)
                        nc.vector.scalar_tensor_tensor(by_block(top, 0), sink, 1.0 / SCALE, smax[:, :, 0], ALU.mult, ALU.max)\
                            .then_inc(soft_step, 1)
                        nc.vector.scalar_tensor_tensor(by_block(top, 1), sink, 1.0 / SCALE, smax[:, :, 2], ALU.mult, ALU.max)\
                            .then_inc(soft_step, 1)
                        soft(3)
                        nc.vector.tensor_tensor(by_block(top, 0), by_block(top, 0), smax[:, :, 1], ALU.max).then_inc(soft_step, 1)
                        soft(4)
                        nc.vector.tensor_scalar(bias, top, -SCALE, None, ALU.mult).then_inc(soft_step, 1)
                        soft(5)
                        for blk in range(2):
                            nc.vector.tensor_tensor(by_block(sink_part, blk), by_block(bias, blk), sink, ALU.add)\
                                .then_inc(bias_made if blk else soft_step, 1)
                        refill(i, 16, base, range(8 * pp + 1, 8 * pp + 2), SLIM)
                        dve.wait_ge(exp_made, i * 2 + (first_head // 4 + pp + 1))
                        nc.vector.tensor_tensor(denom, sums, sink_part, ALU.add).then_inc(soft_step, 1)
                        soft(7)
                        nc.vector.reciprocal(denom, denom).then_inc(merged, 1)
                        dve.wait_ge(merged, i * MERGED[name][1] + (MERGED[name][0] + MERGED[name][1] // 2 * pp + 1))
                        for hh in range(4):
                            nc.vector.tensor_scalar(s_buf[:, hh, 0:T], s_buf[:, hh, 0:T], denom[:, 2 * hh:2 * hh + 1], None, ALU.mult)
                            nc.vector.tensor_scalar(s_buf[:, hh, T:3 * P], s_buf[:, hh, T:3 * P], denom[:, 2 * hh + 1:2 * hh + 2], None,
                                                    ALU.mult).then_inc(probs_made, 1)

                        def take_o(pair):
                            dve.wait_ge(o_hi, i * 4 + (first_head // 2 + 2 * pp + pair + 1))
                            tile = i * 4 + (first_head // 2 + 2 * pp + pair)
                            nc.vector.tensor_tensor(o_t[:, ds(tile, 1), 1, :].rearrange("p a t -> p (a t)"),
                                                    o_bank[pair][:, 0:T],
                                                    o_t[:, ds(tile, 1), 0, :].rearrange("p a t -> p (a t)").bitcast(F32),
                                                    ALU.subtract).then_inc(o_lo, 1)

                        refill(i, 16, base, range(8 * pp + 2, 8 * pp + 7), SLIM)
                        take_o(0)
                        refill(i, 16, base, range(8 * pp + 7, 8 * pp + 8), SLIM)
                        take_o(1)
                        if name == "gr":
                            dve.wait_ge(acc_free, i * 2 + (PANELS[name] + pp + 3))
                            nc.vector.tensor_tensor(merge[:, ds(i * 8 + 4 * pp, 4), :], merge[:, ds(i * 8 + 4 * pp, 4), :],
                                                    gate_sig, ALU.mult).then_inc(merged, 1)

            with dve.Fori(0, 2) as i:
                for pp in range(2):
                    refill(i, 16, UNITS["attn"], range(8 * pp, 8 * pp + 8), SLIM)
                    dve.wait_ge(unit_used, i * 16 + (UNITS["attn"] + 8 * pp + 8))
                    for b in range(2):
                        nc.vector.tensor_tensor(mix_raw[:, 2 * b:2 * b + 2, :],
                                                acc_of("attn", pp)[b][:, :].rearrange("p (k t) -> p k t", k=2),
                                                g_attn[:, ds(i * 8 + (4 * pp + 2 * b), 2), :], ALU.mult)\
                            .then_inc(acc_free if b else attn_gated, 1)
                    dve.wait_ge(attn_gated, i * 2 + (pp + 1))
                    dve.wait_ge(acc_free, i * 2 + (PANELS["attn"] + pp + 3))
                    nc.vector.tensor_tensor(mix_raw[:, :, :], mix_raw[:, :, :], merge[:, ds(i * 8 + 4 * pp, 4), :], ALU.add)\
                        .then_inc(mix_sum, 1)
                    dve.wait_ge(mix_hi, i * 2 + (pp + 1))
                    nc.vector.tensor_tensor(act_t[:, ds(i * 8 + 4 * pp, 4), 1, :], mix_raw[:, :, :],
                                            act_t[:, ds(i * 8 + 4 * pp, 4), 0, :].bitcast(F32), ALU.subtract).then_inc(mix_lo, 1)

            def add_residual(i, name, pp, n_units, scale, steps_before, panels_before):
                dve.wait_ge(unit_used, i * (2 * n_units) + (UNITS[name] + n_units * (pp + 1)))
                for t in range(TOK):
                    part = res[:, t, ds(i * 1024 + 512 * pp, 512)]
                    nc.vector.scalar_tensor_tensor(part, part, scale, acc_of(name, pp)[t][:, :], ALU.mult, ALU.add)\
                        .then_inc(acc_free if t else res_step, 1)

            def panel_stats(i, name, pp, step0):
                dve.wait_ge(res_step, i * 2 + (step0 + pp + 1))
                dve.wait_ge(acc_free, i * 2 + (PANELS[name] + pp + 3))
                for t in range(TOK):
                    nc.vector.bn_stats(stats[:, t, ds(i * 2 + pp, 1), :].rearrange("p a s -> p (a s)"),
                                       res[:, t, ds(i * 1024 + 512 * pp, 512)]).then_inc(stat_step, 1)

            dve.wait_ge(res_loaded, 32)
            with dve.Fori(0, 2) as i:
                for pp in range(2):
                    refill(i, 16, UNITS["out"], range(8 * pp, 8 * pp + 8), SLIM)
                    add_residual(i, "out", pp, 8, ALPHA, 0, 0)
                    panel_stats(i, "out", pp, 0)

            def layer_norm(count):
                n = [count]

                def step(ins, wait=True):
                    ins.then_inc(ln_step, 1)
                    n[0] += 1
                    if wait:
                        dve.wait_ge(ln_step, n[0])

                dve.wait_ge(stat_step, 8 if count == 0 else 16)
                for t in range(TOK):
                    step(nc.vector.bn_aggr(lnv[:, t, 0:2], stats[:, t, :, :].rearrange("p a s -> p (a s)")))
                    step(nc.vector.tensor_scalar(lnv[:, t, 1:2], lnv[:, t, 1:2], LN_EPS, None, ALU.add), wait=False)
                    assert n[0] - count == LN_VAR[t]
                dve.wait_ge(ln_loaded, 32 if count == 0 else 64)
                for t in range(TOK):
                    dve.wait_ge(ln_root, t + 1 + (TOK if count else 0))
                    step(nc.vector.reciprocal(lnv[:, t, 3:4], lnv[:, t, 2:3]))
                    step(nc.vector.tensor_scalar(res[:, t, :], res[:, t, :], lnv[:, t, 0:1], lnv[:, t, 3:4], ALU.subtract, ALU.mult))
                    step(nc.vector.tensor_tensor(res[:, t, :], res[:, t, :], ln_gb[:, 0, :], ALU.mult))
                    step(nc.vector.tensor_tensor(res[:, t, :], res[:, t, :], ln_gb[:, 1, :], ALU.add), wait=False)
                    assert n[0] - count == LN_DONE[t]
                assert n[0] - count == LN_STEPS

            layer_norm(0)
            for kt in range(0, KT, 2):
                dve.wait_ge(ln_hi, kt // 2 + 1)
                nc.vector.tensor_tensor(act_t[:, kt:kt + 2, 1, :], bank[kt // 2][:, :].rearrange("p (k t) -> p k t", k=2),
                                        act_t[:, kt:kt + 2, 0, :].bitcast(F32), ALU.subtract).then_inc(ln_lo, 1)

            for half in range(2):
                name = f"ff{half}"
                with dve.Fori(0, 6) as i:
                    base = UNITS[name]
                    refill(i, 16, base, range(8), SLIM)
                    dve.wait_ge(unit_used, i * 16 + (base + 8))
                    for k in range(3):
                        if k:
                            dve.wait_ge(ff_conv, i * 11 + (66 * half + 4 * k))
                        for c in range(4):
                            src = acc_of(name, 0)[c // 2][:, c % 2 * T:c % 2 * T + T - k]
                            tap = column(i, 4, PAR_FW + 2 * FT_HALF * (2 - k) + FT_HALF * half + c)
                            if k == 0:
                                done = nc.vector.tensor_scalar(gate_c[:, c, :], src, tap,
                                                               column(i, 4, PAR_FB + FT_HALF * half + c), ALU.mult, ALU.add)
                            else:
                                done = nc.vector.scalar_tensor_tensor(gate_c[:, c, k:T], src, tap, gate_c[:, c, k:T], ALU.mult, ALU.add)
                            done.then_inc(acc_free if k == 2 and c == 3 else ff_conv, 1)
                    refill(i, 16, base, range(8, 16), SLIM)
                    dve.wait_ge(unit_used, i * 16 + (base + 16))
                    dve.wait_ge(ff_gelu, i + (6 * half + 1))
                    for b in range(2):
                        nc.vector.tensor_tensor(f_raw[:, 2 * b:2 * b + 2, :], acc_of(name, 1)[b][:, :].rearrange("p (k t) -> p k t", k=2),
                                                gate_c[:, 2 * b:2 * b + 2, :], ALU.mult).then_inc(acc_free if b else ff_prod, 1)
                    dve.wait_ge(ff_hi, i + (6 * half + 1))
                    nc.vector.tensor_tensor(f_t[:, ds(i * 4, 4), 1, :], f_raw[:, :, :],
                                            f_t[:, ds(i * 4, 4), 0, :].bitcast(F32), ALU.subtract).then_inc(ff_lo, 1)
                name = f"down{half}"
                if half == 0:
                    with dve.Fori(0, 2) as i:
                        for pp in range(2):
                            refill(i, 24, UNITS[name], range(12 * pp, 12 * pp + 12), SLIM)
                            add_residual(i, name, pp, 12, ALPHA, 0, 0)
                else:
                    for pp in range(4):
                        refill(0, 0, UNITS[name], [j for j in range(12 * pp, 12 * pp + 12) if j < 44], SLIM)
                        add_residual(0, name, pp, 12, 1.0, 0, 0)
                        panel_stats(0, name, pp, 8)
            layer_norm(LN_STEPS)


CONV_STEPS = 4 * 19
LN_VAR = [2, 4]
LN_DONE = [8, 12]
LN_STEPS = 12
MERGED = {"gr": (0, 4), "ga": (8, 2)}


_INS = ["x", "w_in", "b_gate", "rnn_conv_w", "rnn_conv_b", "lru_wa", "lru_ba", "lru_wi", "lru_bi",
        "lru_lambda", "attn_sinks", "w_attn_proj", "w_rnn_proj", "w_out", "ln1_g", "ln1_b", "ffn_w_up",
        "ffn_w_gate", "ffn_conv_w", "ffn_conv_b", "ffn_w_down", "ln2_g", "ln2_b"]


def shape_constants():
    import numpy as np

    q = np.arange(P)[:, None]
    k = np.arange(2 * P)[None, :]
    d = P + q - k
    neg = np.where((d >= 0) & (d < P), -d, -1e30).astype(np.float32)
    slopes = (2.0 ** (-8.0 * np.arange(1, NH + 1) / NH) / SCALE).astype(np.float32)
    return np.ascontiguousarray(np.concatenate(
        [np.eye(P, dtype=np.float32), np.broadcast_to(slopes, (P, NH)), neg, neg[:, P:]], axis=1))


def kernel(**inputs):
    import numpy as _np
    import concourse.bacc as _bacc
    from concourse import mybir as _mybir
    from concourse.bass_utils import run_bass_kernel_spmd as _run

    nc = _bacc.Bacc("TRN2", target_bir_lowering=False, num_devices=1)
    arrays = {"in_consts_dram": shape_constants()}
    for name in _INS:
        arrays[f"in_{name}_dram"] = _np.ascontiguousarray(inputs[name])
    args = [nc.dram_tensor(n, a.shape, _mybir.dt.from_np(a.dtype), kind="ExternalInput").ap() for n, a in arrays.items()]
    args.append(nc.dram_tensor("out_0_dram", (1, T, D), _mybir.dt.float32, kind="ExternalOutput").ap())
    layer_kernel(nc, *args)
    r = _run(nc, [arrays], core_ids=[0])
    return r.results[0]["out_0_dram"]
```

```python
from contextlib import ExitStack

import concourse.bass as bass
from concourse import mybir

F32 = mybir.dt.float32
F32R = mybir.dt.float32r
ACT = mybir.ActivationFunctionType
ALU = mybir.AluOpType
AX = mybir.AxisListType

P = 128
T = 256
TOK = T // P
D = 2048
KT = D // P
HD = 64
NH, NKV = 32, 4
D_KV = NKV * HD
D_RNN = 2560
RT = D_RNN // P
RB = 160
GRP = 5
D_FF = 3 * D
FT_HALF = D_FF // P // 2
LN_EPS = 1e-5
ALPHA = 2.0 ** 0.25
LRU_C = 8.0
SCALE = HD ** -0.5

COL_Q, COL_KV, COL_RX = 0, D, D + 2 * D_KV
COL_RY = COL_RX + D_RNN
COL_GA = COL_RY + D_RNN
COL_GR = COL_GA + D

PANELS = {}
_n = 0
for _name, _count in (("rxy", 8), ("q", 4), ("kv", 1), ("rnn", 4), ("gr", 4), ("ga", 4),
                      ("attn", 4), ("out", 4), ("ff0", 12), ("down0", 4), ("ff1", 12), ("down1", 4)):
    PANELS[_name] = _n
    _n += _count
UNITS = {}
_u = 0
for _name, _count in (("rxy", 64), ("q", 32), ("kv", 8), ("rnn", 32), ("gr", 32), ("ga", 32),
                      ("attn", 32), ("out", 32), ("ff0", 96), ("down0", 48), ("ff1", 96), ("down1", 48)):
    UNITS[_name] = _u
    _u += _count
LAST_UNIT = _u

WIDE = 1280
SLIM = 1024

LRU_LO = [0, 0, 1, 2, 3]
LRU_HI = [1, 2, 3, 4, 4]
LRU_AT = [0, 2, 5, 8, 11]
LRU_TILES = 13
LRU_PIECES = []
for _b in range(4):
    for _t in range(GRP):
        _r0, _r1 = max(RB * _b, P * _t), min(RB * _b + RB, P * _t + P)
        if _r0 < _r1:
            LRU_PIECES.append((_b, _r0 - RB * _b, _r1 - _r0, _t))

PAR_BG, PAR_CW, PAR_CB, PAR_BA, PAR_BI, PAR_LAM = 0, 32, 112, 132, 152, 172
PAR_G1, PAR_B1, PAR_FW, PAR_FB = 192, 208, 224, 368
PAR_COLS = 416

CONST_ID, CONST_SLOPE, CONST_COLS = 0, P, P + NH


def layer_kernel(nc, consts, x, w_in, b_gate, rnn_conv_w, rnn_conv_b, lru_wa, lru_ba, lru_wi, lru_bi,
                 lru_lambda, attn_sinks, w_attn_proj, w_rnn_proj, w_out, ln1_g, ln1_b, ffn_w_up,
                 ffn_w_gate, ffn_conv_w, ffn_conv_b, ffn_w_down, ln2_g, ln2_b, out):
    ds = bass.ds

    with ExitStack() as ctx:
        BASE = (nc.sbuf_base + 63) // 64 * 64

        def at(name, offset, shape, dt=F32):
            return nc.alloc_sbuf_tensor_at(name, shape, dt, offset=BASE + offset)

        def sem(name):
            return ctx.enter_context(nc.semaphore(name))

        raw = at("raw", 0, [P, 4, 2 * WIDE])
        w_hi = at("w_hi", 40960, [P, 4, WIDE], F32R)
        w_lo = at("w_lo", 61440, [P, 4, WIDE], F32R)
        raw_tail = at("raw_tail", 0, [P, 4, 2 * WIDE])[:, :, 2 * SLIM:]
        gate_sig = at("gate_sig", 40960, [P, 4, WIDE])[:, :, SLIM:]
        q_now = at("q_now", 61440, [P, 4, WIDE])[:, :, SLIM:]
        k_now = raw_tail[:, 0, 0:T]
        v_now = raw_tail[:, 0, T:T + TOK * HD].rearrange("p (b d) -> p b d", b=TOK)
        probs_t = [raw_tail[:, 1, 0:3 * P], raw_tail[:, 2, 0:3 * P]]
        act_t = at("act_t", 81920, [P, KT, 2, T], F32R)
        SMALL = 81920 + 32768
        const = at("const", SMALL, [P, CONST_COLS])
        par = at("par", SMALL + 640, [P, PAR_COLS])
        sinks = at("sinks", SMALL + 2304, [P, NH])
        coef = at("coef", SMALL + 2432, [P, 9, RT])
        smax = at("smax", SMALL + 3168, [P, 4, 3])
        ssmall = at("ssmall", SMALL + 3232, [P, 5, 8])
        stats = at("stats", SMALL + 3392, [P, TOK, 4, 6])
        lnv = at("lnv", SMALL + 3584, [P, TOK, 6])
        ident = const[:, CONST_ID:CONST_ID + P]
        dist = raw_tail[:, 3, 0:3 * P]
        BIG = SMALL + 3648
        x_tok = at("x_tok", BIG, [P, TOK, D])
        par_rows = at("par_rows", BIG + 16384, [P, 4, P])
        g_t = at("g_t", BIG, [P, RT, 2, T], F32R)
        g_work = at("g_work", BIG, [P, RT, 2, T])
        xc = at("xc", BIG + 40960, [P, GRP, T])
        lru_r = at("lru_r", BIG + 46080, [P, GRP, T])
        lru_i = at("lru_i", BIG + 51200, [P, GRP, T])
        lru_a = at("lru_a", BIG + 56320, [P, GRP, T])
        lru_w = at("lru_w", BIG + 61440, [P, 2, LRU_TILES * P])
        o_t = at("o_t", BIG, [P, KT, 2, T], F32R)
        g_attn = at("g_attn", BIG + 32768, [P, KT, T])
        s_buf = at("s_buf", BIG + 49152, [P, 4, 3 * P])
        mix_raw = at("mix_raw", BIG + 49152, [P, 4, T])
        q_all = at("q_all", BIG + 55296, [P, KT, T])
        k_dup = at("k_dup", BIG + 71680, [P, NKV, T])
        v_all = at("v_all", BIG + 75776, [P, TOK, D_KV])
        merge = at("merge", BIG + 77824, [P, KT, T])
        res = at("res", BIG, [P, TOK, D])
        ln_gb = at("ln_gb", BIG + 16384, [P, 2, D])
        f_t = at("f_t", BIG + 32768, [P, FT_HALF, 2, T], F32R)
        gate_c = at("gate_c", BIG + 81920, [P, 4, T])
        f_raw = at("f_raw", BIG + 86016, [P, 4, T])
        ln_t = at("ln_t", BIG + 32768, [P, KT, T])

        bank = [ctx.enter_context(nc.psum_tensor(f"bank{b}", [P, 512], F32)) for b in range(8)]
        ACC = [[bank[0], bank[1], bank[2]], [bank[3], bank[4], bank[5]]]
        gate_bank = [bank[6], bank[7], bank[0], bank[1], bank[2]]
        s_bank = [bank[6], bank[2], bank[5], bank[7]]
        pt_bank = [bank[2], bank[6]]
        o_bank = [bank[5], bank[7]]

        dist_loaded = sem("dist_loaded")
        const_loaded, x_loaded, par_loaded = sem("const_loaded"), [sem(f"x_loaded{n}") for n in range(4)], sem("par_loaded")
        lru_zeroed, lru_w_loaded = sem("lru_zeroed"), sem("lru_w_loaded")
        par_turned, par_made, coef_step, coef_exp = sem("par_turned"), sem("par_made"), sem("coef_step"), sem("coef_exp")
        x_turned, x_hi_made, x_lo_made = sem("x_turned"), sem("x_hi_made"), sem("x_lo_made")
        raw_loaded = [sem(f"raw_loaded{s}") for s in range(4)]
        hi_made, lo_made, unit_used = sem("hi_made"), sem("lo_made"), sem("unit_used")
        acc_free = sem("acc_free")
        conv_step = sem("conv_step")
        gates_done, gates_read = sem("gates_done"), sem("gates_read")
        a_made, th_made, v_made, root_made = sem("a_made"), sem("th_made"), sem("v_made"), sem("root_made")
        lru_step, h_made = sem("lru_step"), sem("h_made")
        g_prod, g_hi, g_lo = sem("g_prod"), sem("g_hi"), sem("g_lo")
        staged_qk, staged_v = sem("staged_qk"), sem("staged_v")
        scores_done, scores_taken = sem("scores_done"), sem("scores_taken")
        soft_step, bias_made, exp_made, probs_made = sem("soft_step"), sem("bias_made"), sem("exp_made"), sem("probs_made")
        pt_done, pt_taken, pv_done, o_hi, o_lo = sem("pt_done"), sem("pt_taken"), sem("pv_done"), sem("o_hi"), sem("o_lo")
        merged = sem("merged")
        attn_gated, mix_sum, mix_hi, mix_lo = sem("attn_gated"), sem("mix_sum"), sem("mix_hi"), sem("mix_lo")
        res_loaded, ln_loaded = sem("res_loaded"), sem("ln_loaded")
        res_step, stat_step, ln_step, ln_root = sem("res_step"), sem("stat_step"), sem("ln_step"), sem("ln_root")
        ln_turned, ln_made, ln_hi, ln_lo = sem("ln_turned"), sem("ln_made"), sem("ln_hi"), sem("ln_lo")
        res_made, ln2_cols, ln2_step = sem("res_made"), [sem("ln2_cols0"), sem("ln2_cols1")], sem("ln2_step")
        ln_norm, ln2_norm, ln2_mul = sem("ln_norm"), sem("ln2_norm"), sem("ln2_mul")
        ff_conv, ff_gelu, ff_prod, ff_hi, ff_lo = sem("ff_conv"), sem("ff_gelu"), sem("ff_prod"), sem("ff_hi"), sem("ff_lo")
        out_stored, act_waited = sem("out_stored"), sem("act_waited")

        def load_chunk(sp, w_rows, chunk, kc, width, col, rot, slot, first=False):
            if not first:
                sp.wait_ge(lo_made, rot * 8 + 2 * slot - 6)
            src = w_rows.rearrange("(k p) n -> p k n", p=P)[:, kc * chunk:kc * chunk + kc, ds(col, width)]
            sp.dma_start(raw[:, slot, 0:kc * width].rearrange("p (k n) -> p k n", k=kc), src)\
              .then_inc(raw_loaded[slot], 16)

        def load_panels(sp, w_rows, n, rot, count, kc, width, col):
            for pp in range(count):
                for c in range(4):
                    load_chunk(sp, w_rows, c, kc, width, (n + pp) * width + col, rot + pp, c)

        def split_hi(act, unit, j, size, refill=True):
            slot, chunk = j % 4, j // 2 % 4
            if j % 2 == 0:
                act.wait_ge(raw_loaded[chunk], (unit + j // 8 * 8) * 2 + 16)
            if refill:
                act.wait_ge(unit_used, unit + j - 3)
            half = j % 2 * size
            nc.scalar.activation(w_hi[:, slot, 0:size], raw[:, chunk, half:half + size], ACT.Copy)\
                .then_inc(hi_made, 1)

        def split_lo(dve, unit, j, size):
            slot, chunk, half = j % 4, j // 2 % 4, j % 2 * size
            dve.wait_ge(hi_made, unit + j + 1)
            nc.vector.tensor_tensor(w_lo[:, slot, 0:size], raw[:, chunk, half:half + size],
                                    w_hi[:, slot, 0:size].bitcast(F32), ALU.subtract).then_inc(lo_made, 1)

        PASSES = ((w_hi, 0), (w_hi, 1), (w_lo, 0))

        def panel_features(pe, unit, j0, acc, moving, kc, width, between=lambda j: None, columns=None):
            size = kc * width // 2
            tiles = width // P if columns is None else columns // P
            for j in range(8):
                slot = (j0 + j) % 4
                pe.wait_ge(lo_made, unit + j0 + j + 1)
                last = None
                for c in range(tiles):
                    dst = acc[c // 2][:, c % 2 * T:c % 2 * T + T]
                    for k in range(kc):
                        at_ = k * width + c * P
                        if at_ // size != j % 2:
                            continue
                        kt = j // 2 * kc + k
                        for n, (w, part) in enumerate(PASSES):
                            last = nc.tensor.matmul(dst, w[:, slot, at_ % size:at_ % size + P], moving[:, kt, part, :],
                                                    start=(kt == 0 and n == 0 and c % 2 == 0),
                                                    stop=(j == 7 and n == 2 and kt == 4 * kc - 1), skip_group_check=True)
                if columns is not None:
                    for t in range(TOK):
                        for k in range(kc):
                            at_ = k * width + columns
                            if at_ // size != j % 2:
                                continue
                            kt = j // 2 * kc + k
                            for n, (w, part) in enumerate(((w_hi, 0), (w_lo, 0), (w_hi, 1))):
                                last = nc.tensor.matmul(acc[1][:, t * T:t * T + T], moving[:, kt, part, t * P:t * P + P],
                                                        w[:, slot, at_ % size:at_ % size + width - columns],
                                                        start=(kt == 0 and n == 0 and t == 0),
                                                        stop=(j == 7 and n == 2 and kt == 4 * kc - 1), skip_group_check=True)
                last.then_inc(unit_used, 1)
                between(j)

        def panel_tokens(pe, unit, j0, acc, stationary, chunks, before=lambda j: None):
            for j in range(2 * chunks):
                slot = (j0 + j) % 4
                before(j)
                pe.wait_ge(lo_made, unit + j0 + j + 1)
                for t in range(TOK):
                    for k in range(2):
                        kt = 2 * j + k
                        for n, (w, part) in enumerate(((w_hi, 0), (w_lo, 0), (w_hi, 1))):
                            last = nc.tensor.matmul(acc[t][:, :], stationary[:, kt, part, t * P:t * P + P],
                                                    w[:, slot, k * 512:k * 512 + 512],
                                                    start=(kt == 0 and n == 0),
                                                    stop=(kt == 4 * chunks - 1 and n == 2))
                last.then_inc(unit_used, 1)

        def acc_of(name, pp):
            return ACC[(PANELS[name] + pp) % 2]

        block = ctx.enter_context(nc.Block())

        @block.sync
        def _(sp):
            sp.dma_start(const[:, :], consts[:, 0:CONST_COLS]).then_inc(const_loaded, 16)
            for n in range(4):
                cols, t = n // 2 * (D // 2), n % 2
                sp.dma_start(x_tok[:, t, cols:cols + D // 2], x[0, t * P:t * P + P, cols:cols + D // 2]).then_inc(x_loaded[n], 16)
            for c in range(4):
                load_chunk(sp, w_in[0], c, 4, 640, COL_RX, 0, c, first=True)

            def load_lru(g):
                for m, w in enumerate((lru_wa, lru_wi)):
                    for b, r0, n, t in LRU_PIECES:
                        row = RB * b + r0 - P * t
                        col = LRU_AT[t] * P + RB * b - LRU_LO[t] * P
                        sp.dma_start(lru_w[row:row + n, m, col:col + RB], w[0, ds(g * 4 + b, 1), r0:r0 + n, :]
                                     .rearrange("a r c -> (a r) c")).then_inc(lru_w_loaded, 16)

            sp.wait_ge(lru_zeroed, 1)
            load_lru(0)
            load_panels(sp, w_in[0], 0, 1, 1, 4, 640, COL_RY)
            with sp.Fori(1, 4) as n:
                load_panels(sp, w_in[0], n, n * 2, 1, 4, 640, COL_RX)
                sp.wait_ge(gates_done, n * GRP)
                load_lru(n)
                load_panels(sp, w_in[0], n, n * 2 + 1, 1, 4, 640, COL_RY)
            with sp.Fori(0, 5) as n:
                load_panels(sp, w_in[0], n, n + PANELS["q"], 1, 4, 512, COL_Q)
            with sp.Fori(0, 4) as n:
                load_panels(sp, w_rnn_proj[0], n, n + PANELS["rnn"], 1, 5, 512, 0)
            load_panels(sp, w_in[0], 0, PANELS["gr"], 1, 4, 512, COL_GR)
            sp.dma_start(dist, consts[:, CONST_COLS:CONST_COLS + 3 * P]).then_inc(dist_loaded, 16)
            with sp.Fori(1, 4) as n:
                load_panels(sp, w_in[0], n, n + PANELS["gr"], 1, 4, 512, COL_GR)
            with sp.Fori(0, 4) as n:
                load_panels(sp, w_in[0], n, n + PANELS["ga"], 1, 4, 512, COL_GA)
            with sp.Fori(0, 4) as n:
                load_panels(sp, w_attn_proj[0], n, n + PANELS["attn"], 1, 4, 512, 0)
            load_panels(sp, w_out[0], 0, PANELS["out"], 1, 4, 512, 0)
            sp.wait_ge(mix_sum, 4)
            for t in range(TOK):
                sp.dma_start(res[:, t, :], x[0, t * P:t * P + P, :]).then_inc(res_loaded, 16)
            for n, v in enumerate((ln1_g, ln1_b)):
                sp.dma_start(ln_gb[:, n, :], v[0].partition_broadcast(P)).then_inc(ln_loaded, 16)
            with sp.Fori(1, 4) as n:
                load_panels(sp, w_out[0], n, n + PANELS["out"], 1, 4, 512, 0)
            rot = UNITS["ff0"] // 8
            for half in range(2):
                with sp.Fori(0, 6) as n:
                    col = n * 512 + half * 6 * 512
                    load_panels(sp, ffn_w_gate[0], 0, n * 2 + rot, 1, 4, 512, col)
                    load_panels(sp, ffn_w_up[0], 0, n * 2 + rot + 1, 1, 4, 512, col)
                if half == 0:
                    sp.wait_ge(res_made, 2 * TOK)
                    for n, v in enumerate((ln2_g, ln2_b)):
                        sp.dma_start(ln_gb[:, n, :], v[0].partition_broadcast(P)).then_inc(ln_loaded, 16)
                rot += 12
                w_down = ffn_w_down[0][half * D_FF // 2:(half + 1) * D_FF // 2, :]
                with sp.Fori(0, 2) as n:
                    for c in range(12):
                        load_chunk(sp, w_down, c % 6, 4, 512, n * 1024 + c // 6 * 512, n * 3 + rot + c // 4, c % 4)
                rot += 6
            for n, (t, c0, c1) in enumerate(OUT_PIECES):
                sp.wait_ge(ln2_cols[t], c1 // (D // 4))
                sp.dma_start(out[0, t * P:t * P + P, c0:c1], res[:, t, c0:c1]).then_inc(out_stored, 16)
            sp.wait_ge(out_stored, 16 * len(OUT_PIECES))

        @block.gpsimd
        def _(pool):
            nc.gpsimd.memset(lru_w[:, :, :], 0.0).then_inc(lru_zeroed, 1)
            pool.wait_ge(acc_free, PANELS["kv"] + 3)
            pool.wait_ge(unit_used, UNITS["gr"])
            for g in range(NKV):
                if g:
                    pool.wait_ge(scores_done, 8 * g)
                nc.gpsimd.tensor_copy(q_now[:, 0:2, :], q_all[:, 4 * g:4 * g + 2, :]).then_inc(staged_qk, 1)
                nc.gpsimd.tensor_copy(k_now, k_dup[:, g, :]).then_inc(staged_qk, 1)
                nc.gpsimd.tensor_copy(q_now[:, 2:4, :], q_all[:, 4 * g + 2:4 * g + 4, :]).then_inc(staged_qk, 1)
                if g:
                    pool.wait_ge(pv_done, 8 * g)
                nc.gpsimd.tensor_copy(v_now, v_all[:, :, HD * g:HD * g + HD]).then_inc(staged_v, 1)
            pool.wait_ge(ln_loaded, 32)
            pool.wait_ge(ln_turned, 8)
            for t in range(TOK):
                nc.gpsimd.tensor_tensor(res[:, t, :], res[:, t, :], ln_gb[:, 0, :], ALU.mult).then_inc(res_made, 1)
                pool.wait_ge(res_made, 2 * t + 1)
                nc.gpsimd.tensor_tensor(res[:, t, :], res[:, t, :], ln_gb[:, 1, :], ALU.add).then_inc(res_made, 1)
            pool.wait_ge(ln_loaded, 64)
            for c in range(4):
                part = slice(c * D // 4, (c + 1) * D // 4)
                pool.wait_ge(ln2_norm, c + 1)
                nc.gpsimd.tensor_tensor(res[:, 1, part], res[:, 1, part], ln_gb[:, 0, part], ALU.mult).then_inc(ln2_mul, 1)
                pool.wait_ge(ln2_mul, c + 1)
                nc.gpsimd.tensor_tensor(res[:, 1, part], res[:, 1, part], ln_gb[:, 1, part], ALU.add).then_inc(ln2_cols[1], 1)

        @block.tensor
        def _(pe):
            pe.wait_ge(const_loaded, 16)
            for kt in range(KT):
                for t in range(TOK):
                    if kt % 8 == 0:
                        pe.wait_ge(x_loaded[kt // 8 * 2 + t], 16)
                    turned = nc.tensor.transpose(bank[kt // 2][:, kt % 2 * T + t * P:kt % 2 * T + t * P + P],
                                                 x_tok[:, t, kt * P:kt * P + P], ident)
                if kt % 2:
                    turned.then_inc(x_turned, 1)
            pe.wait_ge(par_loaded, 16 * 12)
            pe.wait_ge(x_lo_made, 8)
            col = 0
            for n, rows_ in enumerate((112, 112, 96, 96)):
                turned = nc.tensor.transpose(bank[7][:, col:col + rows_], par_rows[0:rows_, n, :], ident[0:rows_, 0:rows_])
                col += rows_
            turned.then_inc(par_turned, 1)

            with pe.Fori(0, 4) as i:
                pe.wait_ge(gates_read, i * GRP + 1)
                pe.wait_ge(acc_free, i * 2 + 1)
                panel_features(pe, i * 16, 0, ACC[0], act_t, 4, 640)

                def gates(c):
                    feeds = [t for t in range(GRP) if LRU_LO[t] <= c <= LRU_HI[t]]
                    for m in range(2):
                        for t in feeds:
                            tile = (LRU_AT[t] + c - LRU_LO[t]) * P
                            done = nc.tensor.matmul(gate_bank[c][:, m * T:m * T + T], lru_w[:, m, tile:tile + P],
                                                    xc[:, t, :], start=(t == feeds[0]), stop=(t == feeds[-1]))
                    done.then_inc(gates_done, 1)

                def between(j):
                    if j == 2:
                        pe.wait_ge(lru_w_loaded, i * 256 + 256)
                        pe.wait_ge(conv_step, i * 19 + 19)
                        pe.wait_ge(acc_free, i * 2 + 3)
                        gates(0)
                        gates(1)
                    if j == 3:
                        gates(2)
                        gates(3)
                    if j == 4:
                        gates(4)

                pe.wait_ge(acc_free, i * 2 + 2)
                panel_features(pe, i * 16, 8, ACC[1], act_t, 4, 640, between=between)

            with pe.Fori(0, 2) as i:
                for pp in range(2):
                    pe.wait_ge(acc_free, i * 2 + (PANELS["q"] + pp + 1))
                    if pp == 0:
                        pe.wait_ge(gates_read, 4 * GRP + 1)
                    panel_features(pe, i * 16 + UNITS["q"], 8 * pp, acc_of("q", pp), act_t, 4, 512)
            pe.wait_ge(acc_free, PANELS["kv"] + 1)
            panel_features(pe, UNITS["kv"], 0, acc_of("kv", 0), act_t, 4, 512, columns=D_KV)
            pe.wait_ge(g_lo, 4)
            with pe.Fori(0, 2) as i:
                for pp in range(2):
                    pe.wait_ge(acc_free, i * 2 + (PANELS["rnn"] + pp + 1))
                    panel_features(pe, i * 16 + UNITS["rnn"], 8 * pp, acc_of("rnn", pp), g_t, 5, 512)

            def attention(i, first_head, pp):
                def scores(hh):
                    half = hh % 2 * HD
                    tile = 2 * pp + hh // 2
                    q = q_now[half:half + HD, tile, :]
                    k = k_now[half:half + HD, :]
                    nc.tensor.matmul(s_bank[hh][:, 0:T], q[:, P:T], k, start=True, stop=True)
                    nc.tensor.matmul(s_bank[hh][:, T:3 * P], q[:, 0:P], k[:, 0:P], start=True, stop=True)\
                        .then_inc(scores_done, 1)

                def turn(hh):
                    pe.wait_ge(probs_made, i * 8 + (first_head + 4 * pp + hh + 1))
                    pe.wait_ge(pt_taken, i * 8 + (first_head + 4 * pp + hh + 1))
                    for n, seg in enumerate((2, 0, 1)):
                        turned = nc.tensor.transpose(pt_bank[hh % 2][:, n * P:n * P + P],
                                                     s_buf[:, hh, seg * P:seg * P + P], ident)
                    turned.then_inc(pt_done, 1)

                def values(hh):
                    half = hh % 2 * HD
                    pair = hh // 2
                    if hh % 2 == 0:
                        pe.wait_ge(o_lo, i * 4 + (first_head // 2 + 2 * pp + hh // 2 + 1))
                    pe.wait_ge(pt_taken, i * 8 + (first_head + 4 * pp + hh + 3))
                    nc.tensor.matmul(o_bank[pair][half:half + HD, 0:T], v_now[:, 0, :], probs_t[hh % 2][:, 0:T],
                                     start=True, stop=False, skip_group_check=True)
                    nc.tensor.matmul(o_bank[pair][half:half + HD, P:T], v_now[:, 1, :], probs_t[hh % 2][:, T:3 * P],
                                     start=False, stop=True, skip_group_check=True).then_inc(pv_done, 1)

                def between(j):
                    if j == 0:
                        if pp == 0:
                            pe.wait_ge(staged_qk, i * 3 + (3 * first_head // 8 + 3))
                        pe.wait_ge(o_lo, i * 4 + (first_head // 2 + 2 * pp + 2))
                        for hh in range(4):
                            scores(hh)
                    if j == 4:
                        turn(0)
                    if j == 5:
                        turn(1)
                        if pp == 0:
                            pe.wait_ge(staged_v, i + (first_head // 8 + 1))
                        values(0)
                    if j == 6:
                        turn(2)
                        values(1)
                        turn(3)
                    if j == 7:
                        values(2)
                        values(3)
                return between

            for name, first_head in (("gr", 0), ("ga", 16)):
                with pe.Fori(0, 2) as i:
                    for pp in range(2):
                        pe.wait_ge(acc_free, i * 2 + (PANELS[name] + pp + 1))
                        panel_features(pe, i * 16 + UNITS[name], 8 * pp, acc_of(name, pp), act_t, 4, 512,
                                       between=attention(i, first_head, pp))

            pe.wait_ge(o_lo, NH // 2 + 1)
            with pe.Fori(0, 2) as i:
                for pp in range(2):
                    pe.wait_ge(acc_free, i * 2 + (PANELS["attn"] + pp + 1))
                    panel_features(pe, i * 16 + UNITS["attn"], 8 * pp, acc_of("attn", pp), o_t, 4, 512,
                                   between=lambda j: pe.wait_ge(o_lo, NH // 2 + 2) if j == 6 and pp == 0 else None)

            pe.wait_ge(mix_lo, 3)
            with pe.Fori(0, 2) as i:
                for pp in range(2):
                    pe.wait_ge(acc_free, i * 2 + (PANELS["out"] + pp + 1))
                    panel_tokens(pe, i * 16 + UNITS["out"], 8 * pp, acc_of("out", pp), act_t, 4,
                                 before=lambda j: pe.wait_ge(mix_lo, 4) if j == 6 and pp == 0 else None)

            for kt in range(KT):
                for t in range(TOK):
                    if kt % 4 == 0:
                        pe.wait_ge(ln_norm, kt // 4 * TOK + t + 1)
                    turned = nc.tensor.transpose(bank[LN_BANK[kt // 2]][:, kt % 2 * T + t * P:kt % 2 * T + t * P + P],
                                                 res[:, t, kt * P:kt * P + P], ident)
                if kt % 2:
                    turned.then_inc(ln_turned, 1)

            def as_split(j):
                if j < 7:
                    pe.wait_ge(ln_lo, j + 2)

            pe.wait_ge(ln_lo, 1)
            pe.wait_ge(ln_made, 2)
            for half in range(2):
                with pe.Fori(0, 6) as i:
                    for pp in range(2):
                        pe.wait_ge(acc_free, i * 2 + (PANELS[f"ff{half}"] + pp + 1))
                        panel_features(pe, i * 16 + UNITS[f"ff{half}"], 8 * pp, acc_of(f"ff{half}", pp), act_t, 4, 512,
                                       between=as_split if half == 0 and pp == 0 else lambda j: None)
                pe.wait_ge(ff_lo, 6 * half + 5)
                with pe.Fori(0, 2) as i:
                    for pp in range(2):
                        pe.wait_ge(acc_free, i * 2 + (PANELS[f"down{half}"] + pp + 1))
                        panel_tokens(pe, i * 24 + UNITS[f"down{half}"], 12 * pp, acc_of(f"down{half}", pp), f_t, 6,
                                     before=lambda j: pe.wait_ge(ff_lo, 6 * half + 6) if j == 10 and pp == 0 else None)

        @block.scalar
        def _(act):
            def wait_apart(semaphore, value):
                act.wait_ge(semaphore, value)
                act.sem_inc(act_waited, 1)

            rows = [(0, 0, b_gate[0].rearrange("(t p) -> t p", p=P)),
                    (0, 32, rnn_conv_w[0].rearrange("k (t p) -> (k t) p", p=P))]
            rows += [(1, RT * n, v[0].rearrange("(t p) -> t p", p=P))
                     for n, v in enumerate((rnn_conv_b, lru_ba, lru_bi, lru_lambda))]
            rows += [(1, 4 * RT + KT * n, v[0].rearrange("(t p) -> t p", p=P)) for n, v in enumerate((ln1_g, ln1_b))]
            taps = ffn_conv_w[0].rearrange("k (t p) -> (k t) p", p=P)
            rows += [(2, 0, taps[0:96]), (3, 0, taps[96:144]), (3, 48, ffn_conv_b[0].rearrange("(t p) -> t p", p=P))]
            for n, row, src in rows:
                act.dma_start(par_rows[row:row + src.shape[0], n, :], src).then_inc(par_loaded, 16)
            act.dma_start(sinks[:, :], attn_sinks[0].partition_broadcast(P)).then_inc(par_loaded, 16)
            act.sem_inc(gates_read, 1)
            act.sem_inc(pt_taken, 2)
            for kt in range(0, KT, 2):
                act.wait_ge(x_turned, kt // 2 + 1)
                nc.scalar.activation(act_t[:, kt:kt + 2, 0, :], bank[kt // 2][:, :].rearrange("p (k t) -> p k t", k=2),
                                     ACT.Copy).then_inc(x_hi_made, 1)
            for j in range(4):
                split_hi(act, 0, j, WIDE, refill=False)
            act.wait_ge(coef_step, 2)
            nc.scalar.activation(coef[:, 2, :], coef[:, 1, :], ACT.Exp, scale=-1.0).then_inc(coef_exp, 1)

            def refill(i, stride, base, js, size):
                for j in js:
                    split_hi(act, i * stride + base, j + 4, size)

            def param(col, i, stride, off):
                return par[:, ds(i * stride + (col + off), 1)]

            def recurrence(i, last_size):
                def group(part):
                    return g_work[:, ds(i * GRP, GRP), part, :]

                def gates(c):
                    wait_apart(gates_done, i * GRP + (c + 1))
                    nc.scalar.activation(lru_r[:, c, :], gate_bank[c][:, 0:T], ACT.Sigmoid, bias=param(PAR_BA, i, GRP, c))
                    nc.scalar.activation(lru_i[:, c, :], gate_bank[c][:, T:2 * T], ACT.Sigmoid, bias=param(PAR_BI, i, GRP, c))\
                        .then_inc(gates_read, 1)

                refill(i, 16, 0, range(0, 11), WIDE)
                gates(0)
                gates(1)
                refill(i, 16, 0, range(11, 12), WIDE)
                gates(2)
                gates(3)
                refill(i, 16, 0, range(12, 13), last_size)
                gates(4)
                wait_apart(gates_read, i * GRP + (GRP + 1))
                for c in range(GRP):
                    nc.scalar.activation(lru_a[:, c, :], lru_r[:, c, :], ACT.Exp,
                                         scale=coef[:, 8, ds(i * GRP + c, 1)]).then_inc(a_made, 1)
                for c in range(GRP):
                    nc.scalar.activation(lru_r[:, c, :], lru_r[:, c, :], ACT.Tanh,
                                         scale=coef[:, 7, ds(i * GRP + c, 1)]).then_inc(th_made, 1)
                refill(i, 16, 0, range(13, 14), last_size)
                wait_apart(v_made, i + 1)
                nc.scalar.activation(group(0), group(0), ACT.Sqrt, scale=2.0 ** 64).then_inc(root_made, 1)
                refill(i, 16, 0, range(14, 16), last_size)
                wait_apart(unit_used, i * 16 + 16)
                for c in range(GRP):
                    done = nc.scalar.activation(g_work[:, ds(i * GRP + c, 1), 1, :].rearrange("p a t -> p (a t)"),
                                                ACC[1][c // 2][:, c % 2 * T:c % 2 * T + T], ACT.Gelu_apprx_tanh)
                done.then_inc(acc_free, 1)
                wait_apart(g_prod, i + 1)
                nc.scalar.activation(g_t[:, ds(i * GRP, GRP), 0, :], xc[:, :, :], ACT.Copy).then_inc(g_hi, 1)

            with act.Fori(0, 3) as i:
                recurrence(i, WIDE)
            recurrence(3, SLIM)

            def copy_panel(i, name, pp, dst):
                wait_apart(unit_used, i * 16 + (UNITS[name] + 8 * pp + 8))
                for b in range(2):
                    done = nc.scalar.activation(dst[:, ds(i * 8 + (4 * pp + 2 * b), 2), :],
                                                acc_of(name, pp)[b][:, :].rearrange("p (k t) -> p k t", k=2), ACT.Copy)
                done.then_inc(acc_free, 1)

            with act.Fori(0, 2) as i:
                for pp in range(2):
                    refill(i, 16, UNITS["q"], range(8 * pp, 8 * pp + 8), SLIM)
                    copy_panel(i, "q", pp, q_all)
            refill(0, 0, UNITS["kv"], range(4), SLIM)
            refill(0, 0, UNITS["kv"], range(4, 8), WIDE)
            act.wait_ge(unit_used, UNITS["kv"] + 8)
            acc = acc_of("kv", 0)
            for parity in range(2):
                for half in range(2):
                    nc.scalar.activation(k_dup[HD * half:HD * half + HD, parity::2, :],
                                         acc[0][HD * parity:HD * parity + HD, :].rearrange("p (k t) -> p k t", k=2), ACT.Copy)
            nc.scalar.activation(v_all[:, :, :], acc[1][:, :].rearrange("p (b d) -> p b d", b=TOK), ACT.Copy)\
                .then_inc(acc_free, 1)
            for pp in range(4):
                refill(0, 0, UNITS["rnn"], range(8 * pp, 8 * pp + 4), WIDE)
                refill(0, 0, UNITS["rnn"], range(8 * pp + 4, 8 * pp + 8), WIDE if pp < 3 else SLIM)
                copy_panel(0, "rnn", pp, merge)

            bias = ssmall[:, 0, :]
            sums = ssmall[:, 2, :]
            for name, first_head, col in (("gr", 0, PAR_BG + KT), ("ga", 16, PAR_BG)):
                with act.Fori(0, 2) as i:
                    for pp in range(2):
                        base = UNITS[name]
                        refill(i, 16, base, range(8 * pp, 8 * pp + 2), SLIM)
                        act.wait_ge(bias_made, i * 2 + (first_head // 4 + pp + 1))
                        for hh in range(4):
                            for blk, (c0, c1) in enumerate(((0, T), (T, 3 * P))):
                                nc.scalar.activation(s_buf[:, hh, c0:c1], s_buf[:, hh, c0:c1], ACT.Exp, scale=SCALE,
                                                     bias=bias[:, 2 * hh + blk:2 * hh + blk + 1],
                                                     accum_out=sums[:, 2 * hh + blk:2 * hh + blk + 1])
                        nc.scalar.activation(ssmall[:, 1, :], ssmall[:, 1, :], ACT.Exp).then_inc(exp_made, 1)

                        def take_pt(hh):
                            act.wait_ge(pt_done, i * 8 + (first_head + 4 * pp + hh + 1))
                            nc.scalar.activation(probs_t[hh % 2], pt_bank[hh % 2][:, 0:3 * P], ACT.Copy).then_inc(pt_taken, 1)

                        def take_o(pair):
                            wait_apart(pv_done, i * 8 + (first_head + 4 * pp + 2 * pair + 2))
                            nc.scalar.activation(o_t[:, ds(i * 4 + (first_head // 2 + 2 * pp + pair), 1), 0, :]
                                                 .rearrange("p a t -> p (a t)"),
                                                 o_bank[pair][:, 0:T], ACT.Copy).then_inc(o_hi, 1)

                        refill(i, 16, base, range(8 * pp + 2, 8 * pp + 5), SLIM)
                        take_pt(0)
                        refill(i, 16, base, range(8 * pp + 5, 8 * pp + 6), SLIM)
                        take_pt(1)
                        refill(i, 16, base, range(8 * pp + 6, 8 * pp + 7), SLIM)
                        act.wait_ge(pv_done, i * 8 + (first_head + 4 * pp + 1))
                        take_pt(2)
                        act.wait_ge(pv_done, i * 8 + (first_head + 4 * pp + 2))
                        take_pt(3)
                        take_o(0)
                        refill(i, 16, base, range(8 * pp + 7, 8 * pp + 8), SLIM)
                        take_o(1)
                        wait_apart(unit_used, i * 16 + (base + 8 * pp + 8))
                        for c in range(4):
                            dst = gate_sig[:, c, :] if name == "gr" else \
                                g_attn[:, ds(i * 8 + (4 * pp + c), 1), :].rearrange("p a t -> p (a t)")
                            done = nc.scalar.activation(dst, acc_of(name, pp)[c // 2][:, c % 2 * T:c % 2 * T + T], ACT.Sigmoid,
                                                        bias=param(col, i, 8, 4 * pp + c))
                        done.then_inc(acc_free, 1)

            with act.Fori(0, 2) as i:
                for pp in range(2):
                    refill(i, 16, UNITS["attn"], range(8 * pp, 8 * pp + 8), SLIM)
                    wait_apart(mix_sum, i * 2 + (pp + 1))
                    nc.scalar.activation(act_t[:, ds(i * 8 + 4 * pp, 4), 0, :], mix_raw[:, :, :], ACT.Copy).then_inc(mix_hi, 1)
            with act.Fori(0, 2) as i:
                refill(i, 16, UNITS["out"], range(16), SLIM)

            act.wait_ge(ln_step, LN_VAR)
            nc.scalar.activation(lnv[:, :, 2], lnv[:, :, 1], ACT.Sqrt).then_inc(ln_root, 1)
            for kt in range(0, KT, 2):
                act.wait_ge(ln_made, kt // 2 + 1)
                nc.scalar.activation(act_t[:, kt:kt + 2, 0, :], ln_t[:, kt:kt + 2, :], ACT.Copy).then_inc(ln_hi, 1)
            for half in range(2):
                with act.Fori(0, 6) as i:
                    base = UNITS[f"ff{half}"]
                    refill(i, 16, base, range(8), SLIM)
                    refill(i, 16, base, range(8, 12), SLIM)
                    act.wait_ge(acc_free, i * 2 + (PANELS[f"ff{half}"] + 3))
                    nc.scalar.activation(gate_c[:, :, :], gate_c[:, :, :], ACT.Gelu_apprx_tanh).then_inc(ff_gelu, 1)
                    refill(i, 16, base, range(12, 16), SLIM)
                    wait_apart(acc_free, i * 2 + (PANELS[f"ff{half}"] + 4))
                    nc.scalar.activation(f_t[:, ds(i * 4, 4), 0, :], f_raw[:, :, :], ACT.Copy).then_inc(ff_hi, 1)
                if half == 0:
                    with act.Fori(0, 2) as i:
                        refill(i, 24, UNITS["down0"], range(24), SLIM)
                else:
                    refill(0, 0, UNITS["down1"], range(44), SLIM)
            act.wait_ge(ln_step, LN_STEPS + LN_VAR)
            nc.scalar.activation(lnv[:, :, 2], lnv[:, :, 1], ACT.Sqrt).then_inc(ln_root, 1)
            act.wait_ge(ln_step, 2 * LN_STEPS)
            for c in range(4):
                part = res[:, 1, c * D // 4:(c + 1) * D // 4]
                nc.scalar.activation(part, part, ACT.Identity, scale=lnv[:, 1, 3:4], bias=lnv[:, 1, 4:5]).then_inc(ln2_norm, 1)

        @block.vector
        def _(dve):
            dve.sem_inc(acc_free, 2)
            dve.sem_inc(o_lo, 2)
            for kt in range(0, KT, 2):
                dve.wait_ge(x_hi_made, kt // 2 + 1)
                nc.vector.tensor_tensor(act_t[:, kt:kt + 2, 1, :], bank[kt // 2][:, :].rearrange("p (k t) -> p k t", k=2),
                                        act_t[:, kt:kt + 2, 0, :].bitcast(F32), ALU.subtract).then_inc(x_lo_made, 1)
            for j in range(4):
                split_lo(dve, 0, j, WIDE)
            dve.wait_ge(par_turned, 1)
            nc.vector.tensor_copy(par[:, :], bank[7][:, 0:PAR_COLS]).then_inc(par_made, 1)
            dve.wait_ge(par_made, 1)

            steps = [0]

            def step(ins):
                ins.then_inc(coef_step, 1)
                steps[0] += 1
                dve.wait_ge(coef_step, steps[0])

            lam = par[:, PAR_LAM:PAR_LAM + RT]
            neg, mag, e, s, s2, poly, low = (coef[:, n, :] for n in range(7))
            step(nc.vector.tensor_scalar(neg, lam, -1.0, None, ALU.mult))
            step(nc.vector.tensor_tensor(mag, neg, lam, ALU.max))
            step(nc.vector.tensor_scalar(low, neg, 0.0, None, ALU.max))
            dve.wait_ge(coef_exp, 1)
            step(nc.vector.tensor_scalar(s2, e, 2.0, None, ALU.add))
            step(nc.vector.reciprocal(s2, s2))
            step(nc.vector.tensor_tensor(s, e, s2, ALU.mult))
            step(nc.vector.tensor_tensor(s2, s, s, ALU.mult))
            step(nc.vector.tensor_scalar(poly, s2, 1.0 / 17, None, ALU.mult))
            for n in (15, 13, 11, 9, 7, 5, 3):
                step(nc.vector.scalar_tensor_tensor(poly, poly, 1.0 / n, s2, ALU.add, ALU.mult))
            step(nc.vector.scalar_tensor_tensor(poly, poly, 1.0, s, ALU.add, ALU.mult))
            step(nc.vector.scalar_tensor_tensor(poly, poly, 2.0, low, ALU.mult, ALU.add))
            step(nc.vector.tensor_scalar(coef[:, 7, :], poly, LRU_C, None, ALU.mult))
            step(nc.vector.tensor_scalar(coef[:, 8, :], poly, -LRU_C, None, ALU.mult))

            def refill(i, stride, base, js, size):
                for j in js:
                    split_lo(dve, i * stride + base, j + 4, size)

            def column(i, stride, col):
                return par[:, ds(i * stride + col, 1)]

            def recurrence(i, last_size):
                def group(part):
                    return g_work[:, ds(i * GRP, GRP), part, :]

                refill(i, 16, 0, range(8), WIDE)
                dve.wait_ge(unit_used, i * 16 + 8)
                for k in range(4):
                    if k:
                        dve.wait_ge(conv_step, i * 19 + 5 * k)
                    for c in range(GRP):
                        src = ACC[0][c // 2][:, c % 2 * T:c % 2 * T + T - k]
                        tap = column(i, GRP, PAR_CW + RT * (3 - k) + c)
                        if k == 0:
                            done = nc.vector.tensor_scalar(xc[:, c, :], src, tap, column(i, GRP, PAR_CB + c), ALU.mult, ALU.add)
                        else:
                            done = nc.vector.scalar_tensor_tensor(xc[:, c, k:T], src, tap, xc[:, c, k:T], ALU.mult, ALU.add)
                        done.then_inc(acc_free if k == 3 and c == GRP - 1 else conv_step, 1)
                refill(i, 16, 0, range(8, 12), WIDE)
                refill(i, 16, 0, range(12, 13), last_size)
                dve.wait_ge(gates_read, i * GRP + (GRP + 1))
                nc.vector.tensor_tensor(lru_i[:, :, :], lru_i[:, :, :], xc[:, :, :], ALU.mult).then_inc(lru_step, 1)
                dve.wait_ge(a_made, i * GRP + GRP)
                nc.vector.tensor_tensor(group(0), lru_a[:, :, :], lru_a[:, :, :], ALU.mult).then_inc(lru_step, 1)
                dve.wait_ge(th_made, i * GRP + GRP)
                dve.wait_ge(lru_step, i * 3 + 2)
                nc.vector.scalar_tensor_tensor(group(0), group(0), 1.0, lru_r[:, :, :], ALU.add, ALU.mult).then_inc(v_made, 1)
                refill(i, 16, 0, range(13, 14), last_size)
                dve.wait_ge(root_made, i + 1)
                nc.vector.scalar_tensor_tensor(lru_i[:, :, :], group(0), 2.0 ** -32, lru_i[:, :, :], ALU.mult, ALU.mult)\
                    .then_inc(lru_step, 1)
                dve.wait_ge(lru_step, i * 3 + 3)
                for c in range(GRP):
                    nc.vector.tensor_tensor_scan(xc[:, c, :], lru_a[:, c, :], lru_i[:, c, :], 0.0, ALU.mult, ALU.add)\
                        .then_inc(h_made, 1)
                refill(i, 16, 0, range(14, 16), last_size)
                dve.wait_ge(acc_free, i * 2 + 4)
                dve.wait_ge(h_made, i * GRP + GRP)
                nc.vector.tensor_tensor(xc[:, :, :], xc[:, :, :], group(1), ALU.mult).then_inc(g_prod, 1)
                dve.wait_ge(g_hi, i + 1)
                nc.vector.tensor_tensor(g_t[:, ds(i * GRP, GRP), 1, :], xc[:, :, :],
                                        g_t[:, ds(i * GRP, GRP), 0, :].bitcast(F32), ALU.subtract).then_inc(g_lo, 1)

            with dve.Fori(0, 3) as i:
                recurrence(i, WIDE)
            recurrence(3, SLIM)

            with dve.Fori(0, 2) as i:
                refill(i, 16, UNITS["q"], range(16), SLIM)
            refill(0, 0, UNITS["kv"], range(4), SLIM)
            refill(0, 0, UNITS["kv"], range(4, 8), WIDE)
            refill(0, 0, UNITS["rnn"], range(28), WIDE)
            refill(0, 0, UNITS["rnn"], range(28, 32), SLIM)

            bias, sink_part, sums = ssmall[:, 0, :], ssmall[:, 1, :], ssmall[:, 2, :]
            denom, top = ssmall[:, 3, :], ssmall[:, 4, :]

            def by_block(tile, blk):
                return tile.rearrange("p (h b) -> p h b", b=2)[:, :, blk]

            SOFT = 7
            for name, first_head in (("gr", 0), ("ga", 16)):
                with dve.Fori(0, 2) as i:
                    for pp in range(2):
                        base = UNITS[name]

                        def soft(n):
                            dve.wait_ge(soft_step, i * (2 * SOFT) + (SOFT * (first_head // 4 + pp) + n))

                        sink = sinks[:, ds(i * 8 + (first_head + 4 * pp), 4)]
                        refill(i, 16, base, range(8 * pp, 8 * pp + 1), SLIM)
                        dve.wait_ge(dist_loaded, 16)
                        for hh in range(4):
                            dve.wait_ge(scores_done, i * 8 + (first_head + 4 * pp + hh + 1))
                            nc.vector.scalar_tensor_tensor(
                                s_buf[:, hh, :], dist, const[:, ds(i * 8 + (CONST_SLOPE + first_head + 4 * pp + hh), 1)],
                                s_bank[hh][:, 0:3 * P], ALU.mult, ALU.add).then_inc(scores_taken, 1)
                        dve.wait_ge(scores_taken, i * 8 + (first_head + 4 * pp + 4))
                        nc.vector.tensor_reduce(smax[:, :, :], s_buf[:, :, :].rearrange("p h (s k) -> p h s k", s=3), AX.X, ALU.max)\
                            .then_inc(soft_step, 1)
                        soft(1)
                        nc.vector.scalar_tensor_tensor(by_block(top, 0), sink, 1.0 / SCALE, smax[:, :, 0], ALU.mult, ALU.max)\
                            .then_inc(soft_step, 1)
                        nc.vector.scalar_tensor_tensor(by_block(top, 1), sink, 1.0 / SCALE, smax[:, :, 2], ALU.mult, ALU.max)\
                            .then_inc(soft_step, 1)
                        soft(3)
                        nc.vector.tensor_tensor(by_block(top, 0), by_block(top, 0), smax[:, :, 1], ALU.max).then_inc(soft_step, 1)
                        soft(4)
                        nc.vector.tensor_scalar(bias, top, -SCALE, None, ALU.mult).then_inc(soft_step, 1)
                        soft(5)
                        for blk in range(2):
                            nc.vector.tensor_tensor(by_block(sink_part, blk), by_block(bias, blk), sink, ALU.add)\
                                .then_inc(bias_made if blk else soft_step, 1)
                        refill(i, 16, base, range(8 * pp + 1, 8 * pp + 2), SLIM)
                        dve.wait_ge(exp_made, i * 2 + (first_head // 4 + pp + 1))
                        nc.vector.tensor_tensor(denom, sums, sink_part, ALU.add).then_inc(soft_step, 1)
                        soft(7)
                        nc.vector.reciprocal(denom, denom).then_inc(merged, 1)
                        dve.wait_ge(merged, i * MERGED[name][1] + (MERGED[name][0] + MERGED[name][1] // 2 * pp + 1))
                        for hh in range(4):
                            nc.vector.tensor_scalar(s_buf[:, hh, 0:T], s_buf[:, hh, 0:T], denom[:, 2 * hh:2 * hh + 1], None, ALU.mult)
                            nc.vector.tensor_scalar(s_buf[:, hh, T:3 * P], s_buf[:, hh, T:3 * P], denom[:, 2 * hh + 1:2 * hh + 2], None,
                                                    ALU.mult).then_inc(probs_made, 1)

                        def take_o(pair):
                            dve.wait_ge(o_hi, i * 4 + (first_head // 2 + 2 * pp + pair + 1))
                            tile = i * 4 + (first_head // 2 + 2 * pp + pair)
                            nc.vector.tensor_tensor(o_t[:, ds(tile, 1), 1, :].rearrange("p a t -> p (a t)"),
                                                    o_bank[pair][:, 0:T],
                                                    o_t[:, ds(tile, 1), 0, :].rearrange("p a t -> p (a t)").bitcast(F32),
                                                    ALU.subtract).then_inc(o_lo, 1)

                        refill(i, 16, base, range(8 * pp + 2, 8 * pp + 7), SLIM)
                        take_o(0)
                        refill(i, 16, base, range(8 * pp + 7, 8 * pp + 8), SLIM)
                        take_o(1)
                        if name == "gr":
                            dve.wait_ge(acc_free, i * 2 + (PANELS[name] + pp + 3))
                            nc.vector.tensor_tensor(merge[:, ds(i * 8 + 4 * pp, 4), :], merge[:, ds(i * 8 + 4 * pp, 4), :],
                                                    gate_sig, ALU.mult).then_inc(merged, 1)

            with dve.Fori(0, 2) as i:
                for pp in range(2):
                    refill(i, 16, UNITS["attn"], range(8 * pp, 8 * pp + 8), SLIM)
                    dve.wait_ge(unit_used, i * 16 + (UNITS["attn"] + 8 * pp + 8))
                    for b in range(2):
                        nc.vector.tensor_tensor(mix_raw[:, 2 * b:2 * b + 2, :],
                                                acc_of("attn", pp)[b][:, :].rearrange("p (k t) -> p k t", k=2),
                                                g_attn[:, ds(i * 8 + (4 * pp + 2 * b), 2), :], ALU.mult)\
                            .then_inc(acc_free if b else attn_gated, 1)
                    dve.wait_ge(attn_gated, i * 2 + (pp + 1))
                    dve.wait_ge(acc_free, i * 2 + (PANELS["attn"] + pp + 3))
                    nc.vector.tensor_tensor(mix_raw[:, :, :], mix_raw[:, :, :], merge[:, ds(i * 8 + 4 * pp, 4), :], ALU.add)\
                        .then_inc(mix_sum, 1)
                    dve.wait_ge(mix_hi, i * 2 + (pp + 1))
                    nc.vector.tensor_tensor(act_t[:, ds(i * 8 + 4 * pp, 4), 1, :], mix_raw[:, :, :],
                                            act_t[:, ds(i * 8 + 4 * pp, 4), 0, :].bitcast(F32), ALU.subtract).then_inc(mix_lo, 1)

            def add_residual(i, name, pp, n_units, scale, steps_before, panels_before):
                dve.wait_ge(unit_used, i * (2 * n_units) + (UNITS[name] + n_units * (pp + 1)))
                for t in range(TOK):
                    part = res[:, t, ds(i * 1024 + 512 * pp, 512)]
                    nc.vector.scalar_tensor_tensor(part, part, scale, acc_of(name, pp)[t][:, :], ALU.mult, ALU.add)\
                        .then_inc(acc_free if t else res_step, 1)

            def panel_stats(i, name, pp, step0):
                dve.wait_ge(res_step, i * 2 + (step0 + pp + 1))
                dve.wait_ge(acc_free, i * 2 + (PANELS[name] + pp + 3))
                for t in range(TOK):
                    nc.vector.bn_stats(stats[:, t, ds(i * 2 + pp, 1), :].rearrange("p a s -> p (a s)"),
                                       res[:, t, ds(i * 1024 + 512 * pp, 512)]).then_inc(stat_step, 1)

            dve.wait_ge(res_loaded, 32)
            with dve.Fori(0, 2) as i:
                for pp in range(2):
                    refill(i, 16, UNITS["out"], range(8 * pp, 8 * pp + 8), SLIM)
                    add_residual(i, "out", pp, 8, ALPHA, 0, 0)
                    panel_stats(i, "out", pp, 0)

            def ln_scales(count):
                dve.wait_ge(stat_step, 8 if count == 0 else 16)
                for t in range(TOK):
                    nc.vector.bn_aggr(lnv[:, t, 0:2], stats[:, t, :, :].rearrange("p a s -> p (a s)")).then_inc(ln_step, 1)
                dve.wait_ge(ln_step, count + 2)
                nc.vector.tensor_scalar(lnv[:, :, 1], lnv[:, :, 1], LN_EPS, None, ALU.add).then_inc(ln_step, 1)
                dve.wait_ge(ln_root, 1 if count == 0 else 2)
                nc.vector.reciprocal(lnv[:, :, 3], lnv[:, :, 2]).then_inc(ln_step, 1)
                dve.wait_ge(ln_step, count + 4)
                nc.vector.scalar_tensor_tensor(lnv[:, :, 4], lnv[:, :, 0], -1.0, lnv[:, :, 3], ALU.mult, ALU.mult)\
                    .then_inc(ln_step, 1)
                dve.wait_ge(ln_step, count + LN_STEPS)

            ln_scales(0)
            for c in range(4):
                for t in range(TOK):
                    part = res[:, t, c * D // 4:(c + 1) * D // 4]
                    nc.vector.tensor_scalar(part, part, lnv[:, t, 0:1], lnv[:, t, 3:4], ALU.subtract, ALU.mult).then_inc(ln_norm, 1)
            for m in range(KT // 2 + 1):
                if m < KT // 2:
                    dve.wait_ge(ln_turned, m + 1)
                    for k in range(2):
                        kt = 2 * m + k
                        done = nc.vector.tensor_scalar(ln_t[:, kt, :], bank[LN_BANK[m]][:, k * T:k * T + T],
                                                       par[:, PAR_G1 + kt:PAR_G1 + kt + 1], par[:, PAR_B1 + kt:PAR_B1 + kt + 1],
                                                       ALU.mult, ALU.add)
                    done.then_inc(ln_made, 1)
                if m:
                    kt = 2 * m - 2
                    dve.wait_ge(ln_hi, m)
                    nc.vector.tensor_tensor(act_t[:, kt:kt + 2, 1, :], ln_t[:, kt:kt + 2, :],
                                            act_t[:, kt:kt + 2, 0, :].bitcast(F32), ALU.subtract).then_inc(ln_lo, 1)

            for half in range(2):
                name = f"ff{half}"
                with dve.Fori(0, 6) as i:
                    base = UNITS[name]
                    refill(i, 16, base, range(8), SLIM)
                    dve.wait_ge(unit_used, i * 16 + (base + 8))
                    for k in range(3):
                        if k:
                            dve.wait_ge(ff_conv, i * 11 + (66 * half + 4 * k))
                        for c in range(4):
                            src = acc_of(name, 0)[c // 2][:, c % 2 * T:c % 2 * T + T - k]
                            tap = column(i, 4, PAR_FW + 2 * FT_HALF * (2 - k) + FT_HALF * half + c)
                            if k == 0:
                                done = nc.vector.tensor_scalar(gate_c[:, c, :], src, tap,
                                                               column(i, 4, PAR_FB + FT_HALF * half + c), ALU.mult, ALU.add)
                            else:
                                done = nc.vector.scalar_tensor_tensor(gate_c[:, c, k:T], src, tap, gate_c[:, c, k:T], ALU.mult, ALU.add)
                            done.then_inc(acc_free if k == 2 and c == 3 else ff_conv, 1)
                    refill(i, 16, base, range(8, 16), SLIM)
                    dve.wait_ge(unit_used, i * 16 + (base + 16))
                    dve.wait_ge(ff_gelu, i + (6 * half + 1))
                    for b in range(2):
                        nc.vector.tensor_tensor(f_raw[:, 2 * b:2 * b + 2, :], acc_of(name, 1)[b][:, :].rearrange("p (k t) -> p k t", k=2),
                                                gate_c[:, 2 * b:2 * b + 2, :], ALU.mult).then_inc(acc_free if b else ff_prod, 1)
                    dve.wait_ge(ff_hi, i + (6 * half + 1))
                    nc.vector.tensor_tensor(f_t[:, ds(i * 4, 4), 1, :], f_raw[:, :, :],
                                            f_t[:, ds(i * 4, 4), 0, :].bitcast(F32), ALU.subtract).then_inc(ff_lo, 1)
                name = f"down{half}"
                if half == 0:
                    dve.wait_ge(res_made, 2 * TOK)
                    with dve.Fori(0, 2) as i:
                        for pp in range(2):
                            refill(i, 24, UNITS[name], range(12 * pp, 12 * pp + 12), SLIM)
                            add_residual(i, name, pp, 12, ALPHA, 0, 0)
                else:
                    for pp in range(4):
                        refill(0, 0, UNITS[name], [j for j in range(12 * pp, 12 * pp + 12) if j < 44], SLIM)
                        add_residual(0, name, pp, 12, 1.0, 0, 0)
                        panel_stats(0, name, pp, 8)
            ln_scales(LN_STEPS)
            dve.wait_ge(ln_loaded, 64)
            for c in range(4):
                cols = slice(c * D // 4, (c + 1) * D // 4)
                part = res[:, 0, cols]
                nc.vector.tensor_scalar(part, part, lnv[:, 0, 0:1], lnv[:, 0, 3:4], ALU.subtract, ALU.mult).then_inc(ln2_step, 1)
                dve.wait_ge(ln2_step, 2 * c + 1)
                nc.vector.tensor_tensor(part, part, ln_gb[:, 0, cols], ALU.mult).then_inc(ln2_step, 1)
                dve.wait_ge(ln2_step, 2 * c + 2)
                nc.vector.tensor_tensor(part, part, ln_gb[:, 1, cols], ALU.add).then_inc(ln2_cols[0], 1)


CONV_STEPS = 4 * 19
LN_STEPS = 5
LN_VAR = 3
LN_BANK = [3, 4, 0, 1, 2, 5, 6, 7]
OUT_PIECES = [(0, 0, D // 2), (1, 0, D // 2), (0, D // 2, D), (1, D // 2, D)]
MERGED = {"gr": (0, 4), "ga": (8, 2)}


_INS = ["x", "w_in", "b_gate", "rnn_conv_w", "rnn_conv_b", "lru_wa", "lru_ba", "lru_wi", "lru_bi",
        "lru_lambda", "attn_sinks", "w_attn_proj", "w_rnn_proj", "w_out", "ln1_g", "ln1_b", "ffn_w_up",
        "ffn_w_gate", "ffn_conv_w", "ffn_conv_b", "ffn_w_down", "ln2_g", "ln2_b"]


def shape_constants():
    import numpy as np

    q = np.arange(P)[:, None]
    k = np.arange(2 * P)[None, :]
    d = P + q - k
    neg = np.where((d >= 0) & (d < P), -d, -1e30).astype(np.float32)
    slopes = (2.0 ** (-8.0 * np.arange(1, NH + 1) / NH) / SCALE).astype(np.float32)
    return np.ascontiguousarray(np.concatenate(
        [np.eye(P, dtype=np.float32), np.broadcast_to(slopes, (P, NH)), neg, neg[:, P:]], axis=1))


def kernel(**inputs):
    import numpy as _np
    import concourse.bacc as _bacc
    from concourse import mybir as _mybir
    from concourse.bass_utils import run_bass_kernel_spmd as _run

    nc = _bacc.Bacc("TRN2", target_bir_lowering=False, num_devices=1)
    arrays = {"in_consts_dram": shape_constants()}
    for name in _INS:
        arrays[f"in_{name}_dram"] = _np.ascontiguousarray(inputs[name])
    args = [nc.dram_tensor(n, a.shape, _mybir.dt.from_np(a.dtype), kind="ExternalInput").ap() for n, a in arrays.items()]
    args.append(nc.dram_tensor("out_0_dram", (1, T, D), _mybir.dt.float32, kind="ExternalOutput").ap())
    layer_kernel(nc, *args)
    r = _run(nc, [arrays], core_ids=[0])
    return r.results[0]["out_0_dram"]
```

```python
from contextlib import ExitStack

import concourse.bass as bass
from concourse import mybir

F32 = mybir.dt.float32
F32R = mybir.dt.float32r
ACT = mybir.ActivationFunctionType
ALU = mybir.AluOpType
AX = mybir.AxisListType

P = 128
T = 256
TOK = T // P
D = 2048
KT = D // P
HD = 64
NH, NKV = 32, 4
D_KV = NKV * HD
D_RNN = 2560
RT = D_RNN // P
RB = 160
GRP = 5
D_FF = 3 * D
FT_HALF = D_FF // P // 2
LN_EPS = 1e-5
ALPHA = 2.0 ** 0.25
LRU_C = 8.0
SCALE = HD ** -0.5

COL_Q, COL_KV, COL_RX = 0, D, D + 2 * D_KV
COL_RY = COL_RX + D_RNN
COL_GA = COL_RY + D_RNN
COL_GR = COL_GA + D

PANELS = {}
_n = 0
for _name, _count in (("rxy", 8), ("q", 4), ("kv", 1), ("rnn", 4), ("gr", 4), ("ga", 4),
                      ("attn", 4), ("out", 4), ("ff0", 12), ("down0", 4), ("ff1", 12), ("down1", 4)):
    PANELS[_name] = _n
    _n += _count
UNITS = {}
_u = 0
for _name, _count in (("rxy", 64), ("q", 32), ("kv", 8), ("rnn", 32), ("gr", 32), ("ga", 32),
                      ("attn", 32), ("out", 32), ("ff0", 96), ("down0", 48), ("ff1", 96), ("down1", 48)):
    UNITS[_name] = _u
    _u += _count
LAST_UNIT = _u

WIDE = 1280
SLIM = 1024

LRU_LO = [0, 0, 1, 2, 3]
LRU_HI = [1, 2, 3, 4, 4]
LRU_AT = [0, 2, 5, 8, 11]
LRU_TILES = 13
LRU_PIECES = []
for _b in range(4):
    for _t in range(GRP):
        _r0, _r1 = max(RB * _b, P * _t), min(RB * _b + RB, P * _t + P)
        if _r0 < _r1:
            LRU_PIECES.append((_b, _r0 - RB * _b, _r1 - _r0, _t))

PAR_BG, PAR_CW, PAR_CB, PAR_BA, PAR_BI, PAR_LAM = 0, 32, 112, 132, 152, 172
PAR_G1, PAR_B1, PAR_FW, PAR_FB = 192, 208, 224, 368
PAR_COLS = 416

CONST_ID, CONST_SLOPE, CONST_COLS = 0, P, P + NH


def layer_kernel(nc, consts, x, w_in, b_gate, rnn_conv_w, rnn_conv_b, lru_wa, lru_ba, lru_wi, lru_bi,
                 lru_lambda, attn_sinks, w_attn_proj, w_rnn_proj, w_out, ln1_g, ln1_b, ffn_w_up,
                 ffn_w_gate, ffn_conv_w, ffn_conv_b, ffn_w_down, ln2_g, ln2_b, out):
    ds = bass.ds

    with ExitStack() as ctx:
        BASE = (nc.sbuf_base + 63) // 64 * 64

        def at(name, offset, shape, dt=F32):
            return nc.alloc_sbuf_tensor_at(name, shape, dt, offset=BASE + offset)

        def sem(name):
            return ctx.enter_context(nc.semaphore(name))

        raw = at("raw", 0, [P, 4, 2 * WIDE])
        w_hi = at("w_hi", 40960, [P, 4, WIDE], F32R)
        w_lo = at("w_lo", 61440, [P, 4, WIDE], F32R)
        raw_tail = at("raw_tail", 0, [P, 4, 2 * WIDE])[:, :, 2 * SLIM:]
        gate_sig = at("gate_sig", 40960, [P, 4, WIDE])[:, :, SLIM:]
        q_now = at("q_now", 61440, [P, 4, WIDE])[:, :, SLIM:]
        k_now = raw_tail[:, 0, 0:T]
        v_now = raw_tail[:, 0, T:T + TOK * HD].rearrange("p (b d) -> p b d", b=TOK)
        probs_t = [raw_tail[:, 1, 0:3 * P], raw_tail[:, 2, 0:3 * P]]
        act_t = at("act_t", 81920, [P, KT, 2, T], F32R)
        SMALL = 81920 + 32768
        const = at("const", SMALL, [P, CONST_COLS])
        par = at("par", SMALL + 640, [P, PAR_COLS])
        sinks = at("sinks", SMALL + 2304, [P, NH])
        coef = at("coef", SMALL + 2432, [P, 9, RT])
        smax = at("smax", SMALL + 3168, [P, 4, 3])
        ssmall = at("ssmall", SMALL + 3232, [P, 5, 8])
        stats = at("stats", SMALL + 3392, [P, TOK, 4, 6])
        lnv = at("lnv", SMALL + 3584, [P, TOK, 6])
        ident = const[:, CONST_ID:CONST_ID + P]
        dist = raw_tail[:, 3, 0:3 * P]
        BIG = SMALL + 3648
        x_tok = at("x_tok", BIG, [P, TOK, D])
        par_rows = at("par_rows", BIG + 16384, [P, 4, P])
        g_t = at("g_t", BIG, [P, RT, 2, T], F32R)
        g_work = at("g_work", BIG, [P, RT, 2, T])
        xc = at("xc", BIG + 40960, [P, GRP, T])
        lru_r = at("lru_r", BIG + 46080, [P, GRP, T])
        lru_i = at("lru_i", BIG + 51200, [P, GRP, T])
        lru_a = at("lru_a", BIG + 56320, [P, GRP, T])
        lru_w = at("lru_w", BIG + 61440, [P, 2, LRU_TILES * P])
        lru_w_lo = at("lru_w_lo", BIG + 61440, [P, 2, LRU_TILES * P], F32R)
        lru_w_hi = at("lru_w_hi", BIG + 74752, [P, 2, LRU_TILES * P], F32R)
        xc_hi = at("xc_hi", BIG + 56320, [P, GRP, T], F32R)
        xc_lo = at("xc_lo", BIG + 88064, [P, GRP, T], F32R)
        o_t = at("o_t", BIG, [P, KT, 2, T], F32R)
        g_attn = at("g_attn", BIG + 32768, [P, KT, T])
        s_buf = at("s_buf", BIG + 49152, [P, 4, 3 * P])
        mix_raw = at("mix_raw", BIG + 49152, [P, 4, T])
        q_all = at("q_all", BIG + 55296, [P, KT, T])
        k_dup = at("k_dup", BIG + 71680, [P, NKV, T])
        v_all = at("v_all", BIG + 75776, [P, TOK, D_KV])
        merge = at("merge", BIG + 77824, [P, KT, T])
        res = at("res", BIG, [P, TOK, D])
        ln_gb = at("ln_gb", BIG + 16384, [P, 2, D])
        f_t = at("f_t", BIG + 32768, [P, FT_HALF, 2, T], F32R)
        gate_c = at("gate_c", BIG + 81920, [P, 4, T])
        f_raw = at("f_raw", BIG + 86016, [P, 4, T])
        ln_t = at("ln_t", BIG + 32768, [P, KT, T])

        bank = [ctx.enter_context(nc.psum_tensor(f"bank{b}", [P, 512], F32)) for b in range(8)]
        ACC = [[bank[0], bank[1], bank[2]], [bank[3], bank[4], bank[5]]]
        gate_bank = [bank[6], bank[7], bank[0], bank[1], bank[2]]
        s_bank = [bank[6], bank[2], bank[5], bank[7]]
        pt_bank = [bank[2], bank[6]]
        o_bank = [bank[5], bank[7]]

        dist_loaded = sem("dist_loaded")
        const_loaded, x_loaded, par_loaded = sem("const_loaded"), [sem(f"x_loaded{n}") for n in range(4)], sem("par_loaded")
        lru_zeroed, lru_w_loaded = sem("lru_zeroed"), sem("lru_w_loaded")
        par_turned, par_made, coef_step, coef_exp = sem("par_turned"), sem("par_made"), sem("coef_step"), sem("coef_exp")
        x_turned, x_hi_made, x_lo_made = sem("x_turned"), sem("x_hi_made"), sem("x_lo_made")
        raw_loaded = [sem(f"raw_loaded{s}") for s in range(4)]
        hi_made, lo_made, unit_used = sem("hi_made"), sem("lo_made"), sem("unit_used")
        acc_free = sem("acc_free")
        conv_step = sem("conv_step")
        lru_w_hi_made, lru_w_lo_made, xc_hi_made, xc_lo_made = sem("lru_w_hi_made"), sem("lru_w_lo_made"), sem("xc_hi_made"), sem("xc_lo_made")
        gates_done, gates_read = sem("gates_done"), sem("gates_read")
        a_made, th_made, v_made, root_made = sem("a_made"), sem("th_made"), sem("v_made"), sem("root_made")
        lru_step, h_made = sem("lru_step"), sem("h_made")
        g_prod, g_hi, g_lo = sem("g_prod"), sem("g_hi"), sem("g_lo")
        staged_qk, staged_v = sem("staged_qk"), sem("staged_v")
        scores_done, scores_taken = sem("scores_done"), sem("scores_taken")
        soft_step, bias_made, exp_made, probs_made = sem("soft_step"), sem("bias_made"), sem("exp_made"), sem("probs_made")
        pt_done, pt_taken, pv_done, o_hi, o_lo = sem("pt_done"), sem("pt_taken"), sem("pv_done"), sem("o_hi"), sem("o_lo")
        merged = sem("merged")
        attn_gated, mix_sum, mix_hi, mix_lo = sem("attn_gated"), sem("mix_sum"), sem("mix_hi"), sem("mix_lo")
        res_loaded, ln_loaded = sem("res_loaded"), sem("ln_loaded")
        res_step, stat_step, ln_step, ln_root = sem("res_step"), sem("stat_step"), sem("ln_step"), sem("ln_root")
        ln_turned, ln_made, ln_hi, ln_lo = sem("ln_turned"), sem("ln_made"), sem("ln_hi"), sem("ln_lo")
        res_made, ln2_done, ln2_step = sem("res_made"), [sem("ln2_done_dve"), sem("ln2_done_pool")], sem("ln2_step")
        ln_norm, ln2_norm, ln2_mul = sem("ln_norm"), sem("ln2_norm"), sem("ln2_mul")
        ff_conv, ff_gelu, ff_prod, ff_hi, ff_lo = sem("ff_conv"), sem("ff_gelu"), sem("ff_prod"), sem("ff_hi"), sem("ff_lo")
        tile0_summed = sem("tile0_summed")
        out_stored, act_waited = sem("out_stored"), sem("act_waited")

        def load_chunk(sp, w_rows, chunk, kc, width, col, rot, slot, first=False):
            if not first:
                sp.wait_ge(lo_made, rot * 8 + 2 * slot - 6)
            src = w_rows.rearrange("(k p) n -> p k n", p=P)[:, kc * chunk:kc * chunk + kc, ds(col, width)]
            sp.dma_start(raw[:, slot, 0:kc * width].rearrange("p (k n) -> p k n", k=kc), src)\
              .then_inc(raw_loaded[slot], 16)

        def load_panels(sp, w_rows, n, rot, count, kc, width, col):
            for pp in range(count):
                for c in range(4):
                    load_chunk(sp, w_rows, c, kc, width, (n + pp) * width + col, rot + pp, c)

        def split_hi(act, unit, j, size, refill=True):
            slot, chunk = j % 4, j // 2 % 4
            if j % 2 == 0:
                act.wait_ge(raw_loaded[chunk], (unit + j // 8 * 8) * 2 + 16)
            if refill:
                act.wait_ge(unit_used, unit + j - 3)
            half = j % 2 * size
            nc.scalar.activation(w_hi[:, slot, 0:size], raw[:, chunk, half:half + size], ACT.Copy)\
                .then_inc(hi_made, 1)

        def split_lo(dve, unit, j, size):
            slot, chunk, half = j % 4, j // 2 % 4, j % 2 * size
            dve.wait_ge(hi_made, unit + j + 1)
            nc.vector.tensor_tensor(w_lo[:, slot, 0:size], raw[:, chunk, half:half + size],
                                    w_hi[:, slot, 0:size].bitcast(F32), ALU.subtract).then_inc(lo_made, 1)

        PASSES = ((w_hi, 0), (w_hi, 1), (w_lo, 0))

        def panel_features(pe, unit, j0, acc, moving, kc, width, between=lambda j: None, columns=None):
            size = kc * width // 2
            tiles = width // P if columns is None else columns // P
            for j in range(8):
                slot = (j0 + j) % 4
                pe.wait_ge(lo_made, unit + j0 + j + 1)
                last = None
                for c in range(tiles):
                    dst = acc[c // 2][:, c % 2 * T:c % 2 * T + T]
                    for k in range(kc):
                        at_ = k * width + c * P
                        if at_ // size != j % 2:
                            continue
                        kt = j // 2 * kc + k
                        for n, (w, part) in enumerate(PASSES):
                            last = nc.tensor.matmul(dst, w[:, slot, at_ % size:at_ % size + P], moving[:, kt, part, :],
                                                    start=(kt == 0 and n == 0 and c % 2 == 0),
                                                    stop=(j == 7 and n == 2 and kt == 4 * kc - 1), skip_group_check=True)
                if columns is not None:
                    for t in range(TOK):
                        for k in range(kc):
                            at_ = k * width + columns
                            if at_ // size != j % 2:
                                continue
                            kt = j // 2 * kc + k
                            for n, (w, part) in enumerate(((w_hi, 0), (w_lo, 0), (w_hi, 1))):
                                last = nc.tensor.matmul(acc[1][:, t * T:t * T + T], moving[:, kt, part, t * P:t * P + P],
                                                        w[:, slot, at_ % size:at_ % size + width - columns],
                                                        start=(kt == 0 and n == 0 and t == 0),
                                                        stop=(j == 7 and n == 2 and kt == 4 * kc - 1), skip_group_check=True)
                last.then_inc(unit_used, 1)
                between(j)

        def panel_tokens(pe, unit, j0, acc, stationary, chunks, before=lambda j: None, tile0_first=False):
            def products(j, t):
                slot = (j0 + j) % 4
                for k in range(2):
                    kt = 2 * j + k
                    for n, (w, part) in enumerate(((w_hi, 0), (w_lo, 0), (w_hi, 1))):
                        last = nc.tensor.matmul(acc[t][:, :], stationary[:, kt, part, t * P:t * P + P],
                                                w[:, slot, k * 512:k * 512 + 512],
                                                start=(kt == 0 and n == 0),
                                                stop=(kt == 4 * chunks - 1 and n == 2))
                return last

            together = 2 * chunks - (4 if tile0_first else 0)
            for j in range(together):
                before(j)
                pe.wait_ge(lo_made, unit + j0 + j + 1)
                products(j, 0)
                products(j, 1).then_inc(unit_used, 1)
            for j in range(together, 2 * chunks):
                before(j)
                pe.wait_ge(lo_made, unit + j0 + j + 1)
                last = products(j, 0)
            if tile0_first:
                last.then_inc(tile0_summed, 1)
            for j in range(together, 2 * chunks):
                products(j, 1).then_inc(unit_used, 1)

        def acc_of(name, pp):
            return ACC[(PANELS[name] + pp) % 2]

        block = ctx.enter_context(nc.Block())

        @block.sync
        def _(sp):
            sp.dma_start(const[:, :], consts[:, 0:CONST_COLS]).then_inc(const_loaded, 16)
            for n in range(4):
                cols, t = n // 2 * (D // 2), n % 2
                sp.dma_start(x_tok[:, t, cols:cols + D // 2], x[0, t * P:t * P + P, cols:cols + D // 2]).then_inc(x_loaded[n], 16)
            for c in range(4):
                load_chunk(sp, w_in[0], c, 4, 640, COL_RX, 0, c, first=True)
            rows = [(0, 0, b_gate[0].rearrange("(t p) -> t p", p=P)),
                    (0, 32, rnn_conv_w[0].rearrange("k (t p) -> (k t) p", p=P))]
            rows += [(1, RT * n, v[0].rearrange("(t p) -> t p", p=P))
                     for n, v in enumerate((rnn_conv_b, lru_ba, lru_bi, lru_lambda))]
            rows += [(1, 4 * RT + KT * n, v[0].rearrange("(t p) -> t p", p=P)) for n, v in enumerate((ln1_g, ln1_b))]
            taps = ffn_conv_w[0].rearrange("k (t p) -> (k t) p", p=P)
            rows += [(2, 0, taps[0:96]), (3, 0, taps[96:144]), (3, 48, ffn_conv_b[0].rearrange("(t p) -> t p", p=P))]
            for n, row, src in rows:
                sp.dma_start(par_rows[row:row + src.shape[0], n, :], src).then_inc(par_loaded, 16)
            sp.dma_start(sinks[:, :], attn_sinks[0].partition_broadcast(P)).then_inc(par_loaded, 16)

            def load_lru(g):
                for m, w in enumerate((lru_wa, lru_wi)):
                    for b, r0, n, t in LRU_PIECES:
                        row = RB * b + r0 - P * t
                        col = LRU_AT[t] * P + RB * b - LRU_LO[t] * P
                        sp.dma_start(lru_w[row:row + n, m, col:col + RB], w[0, ds(g * 4 + b, 1), r0:r0 + n, :]
                                     .rearrange("a r c -> (a r) c")).then_inc(lru_w_loaded, 16)

            sp.wait_ge(lru_zeroed, 1)
            load_lru(0)
            load_panels(sp, w_in[0], 0, 1, 1, 4, 640, COL_RY)
            with sp.Fori(1, 4) as n:
                load_panels(sp, w_in[0], n, n * 2, 1, 4, 640, COL_RX)
                sp.wait_ge(lru_zeroed, n + 1)
                load_lru(n)
                load_panels(sp, w_in[0], n, n * 2 + 1, 1, 4, 640, COL_RY)
            with sp.Fori(0, 5) as n:
                load_panels(sp, w_in[0], n, n + PANELS["q"], 1, 4, 512, COL_Q)
            with sp.Fori(0, 4) as n:
                load_panels(sp, w_rnn_proj[0], n, n + PANELS["rnn"], 1, 5, 512, 0)
            load_panels(sp, w_in[0], 0, PANELS["gr"], 1, 4, 512, COL_GR)
            sp.dma_start(dist, consts[:, CONST_COLS:CONST_COLS + 3 * P]).then_inc(dist_loaded, 16)
            with sp.Fori(1, 4) as n:
                load_panels(sp, w_in[0], n, n + PANELS["gr"], 1, 4, 512, COL_GR)
            with sp.Fori(0, 4) as n:
                load_panels(sp, w_in[0], n, n + PANELS["ga"], 1, 4, 512, COL_GA)
            with sp.Fori(0, 4) as n:
                load_panels(sp, w_attn_proj[0], n, n + PANELS["attn"], 1, 4, 512, 0)
            load_panels(sp, w_out[0], 0, PANELS["out"], 1, 4, 512, 0)
            for c in range(2):
                load_chunk(sp, w_out[0], c, 4, 512, 512, PANELS["out"] + 1, c)
            sp.wait_ge(mix_sum, 4)
            for t in range(TOK):
                sp.dma_start(res[:, t, :], x[0, t * P:t * P + P, :]).then_inc(res_loaded, 16)
            for c in range(2, 4):
                load_chunk(sp, w_out[0], c, 4, 512, 512, PANELS["out"] + 1, c)
            for n, v in enumerate((ln1_g, ln1_b)):
                sp.dma_start(ln_gb[:, n, :], v[0].partition_broadcast(P)).then_inc(ln_loaded, 16)
            with sp.Fori(2, 4) as n:
                load_panels(sp, w_out[0], n, n + PANELS["out"], 1, 4, 512, 0)
            rot = UNITS["ff0"] // 8
            for half in range(2):
                with sp.Fori(0, 6) as n:
                    col = n * 512 + half * 6 * 512
                    load_panels(sp, ffn_w_gate[0], 0, n * 2 + rot, 1, 4, 512, col)
                    load_panels(sp, ffn_w_up[0], 0, n * 2 + rot + 1, 1, 4, 512, col)
                if half == 0:
                    sp.wait_ge(res_made, 2 * TOK)
                    for n, v in enumerate((ln2_g, ln2_b)):
                        sp.dma_start(ln_gb[:, n, :], v[0].partition_broadcast(P)).then_inc(ln_loaded, 16)
                rot += 12
                w_down = ffn_w_down[0][half * D_FF // 2:(half + 1) * D_FF // 2, :]
                with sp.Fori(0, 2) as n:
                    for c in range(12):
                        load_chunk(sp, w_down, c % 6, 4, 512, n * 1024 + c // 6 * 512, n * 3 + rot + c // 4, c % 4)
                rot += 6
            for t, c0, c1, maker, count in OUT_PIECES:
                sp.wait_ge(ln2_done[maker], count)
                sp.dma_start(out[0, t * P:t * P + P, c0:c1], res[:, t, c0:c1]).then_inc(out_stored, 16)
            sp.wait_ge(out_stored, 16 * len(OUT_PIECES))

        @block.gpsimd
        def _(pool):
            nc.gpsimd.memset(lru_w[:, :, :], 0.0).then_inc(lru_zeroed, 1)
            for n in range(1, 4):
                pool.wait_ge(gates_done, n * GRP)
                nc.gpsimd.memset(lru_w[:, :, :], 0.0).then_inc(lru_zeroed, 1)
            pool.wait_ge(acc_free, PANELS["kv"] + 3)
            pool.wait_ge(unit_used, UNITS["gr"] - 2)
            for g in range(NKV):
                if g:
                    pool.wait_ge(scores_done, 8 * g)
                nc.gpsimd.tensor_copy(q_now[:, 0:2, :], q_all[:, 4 * g:4 * g + 2, :]).then_inc(staged_qk, 1)
                nc.gpsimd.tensor_copy(k_now, k_dup[:, g, :]).then_inc(staged_qk, 1)
                if g == 0:
                    pool.wait_ge(unit_used, UNITS["gr"])
                nc.gpsimd.tensor_copy(q_now[:, 2:4, :], q_all[:, 4 * g + 2:4 * g + 4, :]).then_inc(staged_qk, 1)
                if g:
                    pool.wait_ge(pv_done, 8 * g)
                nc.gpsimd.tensor_copy(v_now, v_all[:, :, HD * g:HD * g + HD]).then_inc(staged_v, 1)
            pool.wait_ge(ln_loaded, 32)
            pool.wait_ge(ln_turned, 8)
            for t in range(TOK):
                nc.gpsimd.tensor_tensor(res[:, t, :], res[:, t, :], ln_gb[:, 0, :], ALU.mult).then_inc(res_made, 1)
                pool.wait_ge(res_made, 2 * t + 1)
                nc.gpsimd.tensor_tensor(res[:, t, :], res[:, t, :], ln_gb[:, 1, :], ALU.add).then_inc(res_made, 1)
            pool.wait_ge(ln_loaded, 64)
            for n, (t, c) in enumerate(POOL_PIECES):
                cols = slice(c * D // 4, (c + 1) * D // 4)
                part = res[:, t, cols]
                pool.wait_ge(ln2_norm, n + 1)
                nc.gpsimd.tensor_tensor(part, part, ln_gb[:, 0, cols], ALU.mult).then_inc(ln2_mul, 1)
                pool.wait_ge(ln2_mul, n + 1)
                nc.gpsimd.tensor_tensor(part, part, ln_gb[:, 1, cols], ALU.add).then_inc(ln2_done[1], 1)

        @block.tensor
        def _(pe):
            pe.wait_ge(const_loaded, 16)
            for kt in range(KT):
                for t in range(TOK):
                    if kt % 8 == 0:
                        pe.wait_ge(x_loaded[kt // 8 * 2 + t], 16)
                    turned = nc.tensor.transpose(bank[kt // 2][:, kt % 2 * T + t * P:kt % 2 * T + t * P + P],
                                                 x_tok[:, t, kt * P:kt * P + P], ident)
                if kt % 2:
                    turned.then_inc(x_turned, 1)
            def turn_parameters():
                pe.wait_ge(par_loaded, 16 * 12)
                pe.wait_ge(x_lo_made, 8)
                col = 0
                for n, rows_ in enumerate((112, 112, 96, 96)):
                    turned = nc.tensor.transpose(bank[7][:, col:col + rows_], par_rows[0:rows_, n, :], ident[0:rows_, 0:rows_])
                    col += rows_
                turned.then_inc(par_turned, 1)

            def recurrence(i, during_x=lambda j: None):
                pe.wait_ge(gates_read, i * GRP + 1)
                pe.wait_ge(acc_free, i * 2 + 1)
                panel_features(pe, i * 16, 0, ACC[0], act_t, 4, 640, between=during_x)

                def gates(c):
                    feeds = [t for t in range(GRP) if LRU_LO[t] <= c <= LRU_HI[t]]
                    for m in range(2):
                        for t in feeds:
                            tile = (LRU_AT[t] + c - LRU_LO[t]) * P
                            for n, (w, v) in enumerate(((lru_w_hi, xc_hi), (lru_w_hi, xc_lo), (lru_w_lo, xc_hi))):
                                done = nc.tensor.matmul(gate_bank[c][:, m * T:m * T + T], w[:, m, tile:tile + P], v[:, t, :],
                                                        start=(t == feeds[0] and n == 0), stop=(t == feeds[-1] and n == 2))
                    done.then_inc(gates_done, 1)

                def between(j):
                    if j == 4:
                        pe.wait_ge(lru_w_lo_made, i * 2 + 2)
                        pe.wait_ge(xc_lo_made, i + 1)
                        pe.wait_ge(acc_free, i * 2 + 3)
                        gates(0)
                        gates(1)
                    if j == 5:
                        gates(2)
                        gates(3)
                    if j == 6:
                        gates(4)

                pe.wait_ge(acc_free, i * 2 + 2)
                panel_features(pe, i * 16, 8, ACC[1], act_t, 4, 640, between=between)

            recurrence(0, during_x=lambda j: turn_parameters() if j == 3 else None)
            with pe.Fori(1, 4) as i:
                recurrence(i)

            with pe.Fori(0, 2) as i:
                for pp in range(2):
                    pe.wait_ge(acc_free, i * 2 + (PANELS["q"] + pp + 1))
                    if pp == 0:
                        pe.wait_ge(gates_read, 4 * GRP + 1)
                    panel_features(pe, i * 16 + UNITS["q"], 8 * pp, acc_of("q", pp), act_t, 4, 512)
            pe.wait_ge(acc_free, PANELS["kv"] + 1)
            panel_features(pe, UNITS["kv"], 0, acc_of("kv", 0), act_t, 4, 512, columns=D_KV)
            pe.wait_ge(g_lo, 4)
            with pe.Fori(0, 2) as i:
                for pp in range(2):
                    pe.wait_ge(acc_free, i * 2 + (PANELS["rnn"] + pp + 1))
                    panel_features(pe, i * 16 + UNITS["rnn"], 8 * pp, acc_of("rnn", pp), g_t, 5, 512)

            def attention(i, first_head, pp):
                def scores(hh):
                    half = hh % 2 * HD
                    tile = 2 * pp + hh // 2
                    q = q_now[half:half + HD, tile, :]
                    k = k_now[half:half + HD, :]
                    nc.tensor.matmul(s_bank[hh][:, 0:T], q[:, P:T], k, start=True, stop=True)
                    nc.tensor.matmul(s_bank[hh][:, T:3 * P], q[:, 0:P], k[:, 0:P], start=True, stop=True)\
                        .then_inc(scores_done, 1)

                def turn(hh):
                    pe.wait_ge(probs_made, i * 8 + (first_head + 4 * pp + hh + 1))
                    pe.wait_ge(pt_taken, i * 8 + (first_head + 4 * pp + hh + 1))
                    for n, seg in enumerate((2, 0, 1)):
                        turned = nc.tensor.transpose(pt_bank[hh % 2][:, n * P:n * P + P],
                                                     s_buf[:, hh, seg * P:seg * P + P], ident)
                    turned.then_inc(pt_done, 1)

                def values(hh):
                    half = hh % 2 * HD
                    pair = hh // 2
                    if hh % 2 == 0:
                        pe.wait_ge(o_lo, i * 4 + (first_head // 2 + 2 * pp + hh // 2 + 1))
                    pe.wait_ge(pt_taken, i * 8 + (first_head + 4 * pp + hh + 3))
                    nc.tensor.matmul(o_bank[pair][half:half + HD, 0:T], v_now[:, 0, :], probs_t[hh % 2][:, 0:T],
                                     start=True, stop=False, skip_group_check=True)
                    nc.tensor.matmul(o_bank[pair][half:half + HD, P:T], v_now[:, 1, :], probs_t[hh % 2][:, T:3 * P],
                                     start=False, stop=True, skip_group_check=True).then_inc(pv_done, 1)

                def between(j):
                    if j == 0:
                        pe.wait_ge(staged_qk, i * 3 + (3 * first_head // 8 + 2 + pp))
                        pe.wait_ge(o_lo, i * 4 + (first_head // 2 + 2 * pp + 2))
                        for hh in range(4):
                            scores(hh)
                    if j == 4:
                        turn(0)
                    if j == 5:
                        turn(1)
                        if pp == 0:
                            pe.wait_ge(staged_v, i + (first_head // 8 + 1))
                        values(0)
                    if j == 6:
                        turn(2)
                        values(1)
                        turn(3)
                    if j == 7:
                        values(2)
                        values(3)
                return between

            for name, first_head in (("gr", 0), ("ga", 16)):
                with pe.Fori(0, 2) as i:
                    for pp in range(2):
                        pe.wait_ge(acc_free, i * 2 + (PANELS[name] + pp + 1))
                        panel_features(pe, i * 16 + UNITS[name], 8 * pp, acc_of(name, pp), act_t, 4, 512,
                                       between=attention(i, first_head, pp))

            pe.wait_ge(o_lo, NH // 2 + 1)
            with pe.Fori(0, 2) as i:
                for pp in range(2):
                    pe.wait_ge(acc_free, i * 2 + (PANELS["attn"] + pp + 1))
                    panel_features(pe, i * 16 + UNITS["attn"], 8 * pp, acc_of("attn", pp), o_t, 4, 512,
                                   between=lambda j: pe.wait_ge(o_lo, NH // 2 + 2) if j == 6 and pp == 0 else None)

            pe.wait_ge(mix_lo, 3)
            for pp in range(4):
                pe.wait_ge(acc_free, PANELS["out"] + pp + 1)
                panel_tokens(pe, UNITS["out"], 8 * pp, acc_of("out", pp), act_t, 4,
                             before=lambda j: pe.wait_ge(mix_lo, 4) if j == 6 and pp == 0 else None, tile0_first=pp == 3)

            for t in range(TOK):
                for kt in range(KT):
                    if kt % 4 == 0:
                        pe.wait_ge(ln_norm, 4 * t + kt // 4 + 1)
                    if t == 0 and kt == KT - 2:
                        pe.wait_ge(acc_free, PANELS["out"] + 6)
                    turned = nc.tensor.transpose(bank[LN_BANK[kt // 2]][:, kt % 2 * T + t * P:kt % 2 * T + t * P + P],
                                                 res[:, t, kt * P:kt * P + P], ident)
                    if t and kt % 2:
                        turned.then_inc(ln_turned, 1)

            def as_split(j):
                if j < 7:
                    pe.wait_ge(ln_lo, j + 2)

            pe.wait_ge(ln_lo, 1)
            pe.wait_ge(ln_made, 2)
            for half in range(2):
                with pe.Fori(0, 6) as i:
                    for pp in range(2):
                        pe.wait_ge(acc_free, i * 2 + (PANELS[f"ff{half}"] + pp + 1))
                        panel_features(pe, i * 16 + UNITS[f"ff{half}"], 8 * pp, acc_of(f"ff{half}", pp), act_t, 4, 512,
                                       between=as_split if half == 0 and pp == 0 else lambda j: None)
                pe.wait_ge(ff_lo, 6 * half + 5)
                def last_four(j, pp):
                    if j == 10 and pp == 0:
                        pe.wait_ge(ff_lo, 6 * half + 6)

                if half == 0:
                    with pe.Fori(0, 2) as i:
                        for pp in range(2):
                            pe.wait_ge(acc_free, i * 2 + (PANELS["down0"] + pp + 1))
                            panel_tokens(pe, i * 24 + UNITS["down0"], 12 * pp, acc_of("down0", pp), f_t, 6,
                                         before=lambda j: last_four(j, pp))
                else:
                    for pp in range(4):
                        pe.wait_ge(acc_free, PANELS["down1"] + pp + 1)
                        panel_tokens(pe, UNITS["down1"], 12 * pp, acc_of("down1", pp), f_t, 6,
                                     before=lambda j: last_four(j, pp), tile0_first=pp == 3)

        @block.scalar
        def _(act):
            def wait_apart(semaphore, value):
                act.wait_ge(semaphore, value)
                act.sem_inc(act_waited, 1)

            act.sem_inc(gates_read, 1)
            act.sem_inc(pt_taken, 2)
            for kt in range(0, KT, 2):
                act.wait_ge(x_turned, kt // 2 + 1)
                nc.scalar.activation(act_t[:, kt:kt + 2, 0, :], bank[kt // 2][:, :].rearrange("p (k t) -> p k t", k=2),
                                     ACT.Copy).then_inc(x_hi_made, 1)
            for j in range(4):
                split_hi(act, 0, j, WIDE, refill=False)

            def refill(i, stride, base, js, size):
                for j in js:
                    split_hi(act, i * stride + base, j + 4, size)

            refill(0, 0, 0, range(3), WIDE)
            act.wait_ge(coef_step, 2)
            nc.scalar.activation(coef[:, 2, :], coef[:, 1, :], ACT.Exp, scale=-1.0).then_inc(coef_exp, 1)

            def param(col, i, stride, off):
                return par[:, ds(i * stride + (col + off), 1)]

            def recurrence(i, last_size):
                def group(part):
                    return g_work[:, ds(i * GRP, GRP), part, :]

                def gates(c):
                    wait_apart(gates_done, i * GRP + (c + 1))
                    nc.scalar.activation(lru_r[:, c, :], gate_bank[c][:, 0:T], ACT.Sigmoid, bias=param(PAR_BA, i, GRP, c))
                    nc.scalar.activation(lru_i[:, c, :], gate_bank[c][:, T:2 * T], ACT.Sigmoid, bias=param(PAR_BI, i, GRP, c))\
                        .then_inc(gates_read, 1)

                refill(i, 16, 0, range(3, 5), WIDE)
                act.wait_ge(lru_w_loaded, i * 256 + 256)
                for m in range(2):
                    nc.scalar.activation(lru_w_hi[:, m, :], lru_w[:, m, :], ACT.Copy).then_inc(lru_w_hi_made, 1)
                    refill(i, 16, 0, range(5 + m, 6 + m), WIDE)
                refill(i, 16, 0, range(7, 10), WIDE)
                act.wait_ge(conv_step, i * 19 + 19)
                act.wait_ge(acc_free, i * 2 + 3)
                nc.scalar.activation(xc_hi[:, :, :], xc[:, :, :], ACT.Copy).then_inc(xc_hi_made, 1)
                refill(i, 16, 0, range(10, 12), WIDE)
                refill(i, 16, 0, range(12, 13), last_size)
                gates(0)
                gates(1)
                refill(i, 16, 0, range(13, 14), last_size)
                gates(2)
                gates(3)
                refill(i, 16, 0, range(14, 15), last_size)
                gates(4)
                wait_apart(gates_read, i * GRP + (GRP + 1))
                for c in range(GRP):
                    nc.scalar.activation(lru_a[:, c, :], lru_r[:, c, :], ACT.Exp,
                                         scale=coef[:, 8, ds(i * GRP + c, 1)]).then_inc(a_made, 1)
                for c in range(GRP):
                    nc.scalar.activation(lru_r[:, c, :], lru_r[:, c, :], ACT.Tanh,
                                         scale=coef[:, 7, ds(i * GRP + c, 1)]).then_inc(th_made, 1)
                refill(i, 16, 0, range(15, 16), last_size)
                wait_apart(v_made, i + 1)
                nc.scalar.activation(group(0), group(0), ACT.Sqrt, scale=2.0 ** 64).then_inc(root_made, 1)
                refill(i, 16, 0, range(16, 18), last_size)
                wait_apart(unit_used, i * 16 + 16)
                for c in range(GRP):
                    done = nc.scalar.activation(g_work[:, ds(i * GRP + c, 1), 1, :].rearrange("p a t -> p (a t)"),
                                                ACC[1][c // 2][:, c % 2 * T:c % 2 * T + T], ACT.Gelu_apprx_tanh)
                done.then_inc(acc_free, 1)
                refill(i, 16, 0, range(18, 19), last_size)
                wait_apart(g_prod, i + 1)
                nc.scalar.activation(g_t[:, ds(i * GRP, GRP), 0, :], xc[:, :, :], ACT.Copy).then_inc(g_hi, 1)

            with act.Fori(0, 3) as i:
                recurrence(i, WIDE)
            recurrence(3, SLIM)

            def copy_panel(i, name, pp, dst):
                wait_apart(unit_used, i * 16 + (UNITS[name] + 8 * pp + 8))
                for b in range(2):
                    done = nc.scalar.activation(dst[:, ds(i * 8 + (4 * pp + 2 * b), 2), :],
                                                acc_of(name, pp)[b][:, :].rearrange("p (k t) -> p k t", k=2), ACT.Copy)
                done.then_inc(acc_free, 1)

            with act.Fori(0, 2) as i:
                for pp in range(2):
                    refill(i, 16, UNITS["q"], range(8 if pp else 3, 8 * pp + 8), SLIM)
                    copy_panel(i, "q", pp, q_all)
                refill(i, 16, UNITS["q"], range(16, 19), SLIM)
            refill(0, 0, UNITS["kv"], range(3, 4), SLIM)
            refill(0, 0, UNITS["kv"], range(4, 8), WIDE)
            act.wait_ge(unit_used, UNITS["kv"] + 8)
            acc = acc_of("kv", 0)
            for parity in range(2):
                for half in range(2):
                    nc.scalar.activation(k_dup[HD * half:HD * half + HD, parity::2, :],
                                         acc[0][HD * parity:HD * parity + HD, :].rearrange("p (k t) -> p k t", k=2), ACT.Copy)
            nc.scalar.activation(v_all[:, :, :], acc[1][:, :].rearrange("p (b d) -> p b d", b=TOK), ACT.Copy)\
                .then_inc(acc_free, 1)
            for pp in range(4):
                refill(0, 0, UNITS["rnn"], range(8 * pp, 8 * pp + 4), WIDE)
                refill(0, 0, UNITS["rnn"], range(8 * pp + 4, 8 * pp + 8), WIDE if pp < 3 else SLIM)
                copy_panel(0, "rnn", pp, merge)

            bias = ssmall[:, 0, :]
            sums = ssmall[:, 2, :]
            for name, first_head, col in (("gr", 0, PAR_BG + KT), ("ga", 16, PAR_BG)):
                with act.Fori(0, 2) as i:
                    for pp in range(2):
                        base = UNITS[name]
                        refill(i, 16, base, range(8 * pp, 8 * pp + 2), SLIM)
                        act.wait_ge(bias_made, i * 2 + (first_head // 4 + pp + 1))
                        for hh in range(4):
                            for blk, (c0, c1) in enumerate(((0, T), (T, 3 * P))):
                                nc.scalar.activation(s_buf[:, hh, c0:c1], s_buf[:, hh, c0:c1], ACT.Exp, scale=SCALE,
                                                     bias=bias[:, 2 * hh + blk:2 * hh + blk + 1],
                                                     accum_out=sums[:, 2 * hh + blk:2 * hh + blk + 1])
                        nc.scalar.activation(ssmall[:, 1, :], ssmall[:, 1, :], ACT.Exp).then_inc(exp_made, 1)

                        def take_pt(hh):
                            act.wait_ge(pt_done, i * 8 + (first_head + 4 * pp + hh + 1))
                            nc.scalar.activation(probs_t[hh % 2], pt_bank[hh % 2][:, 0:3 * P], ACT.Copy).then_inc(pt_taken, 1)

                        def take_o(pair):
                            wait_apart(pv_done, i * 8 + (first_head + 4 * pp + 2 * pair + 2))
                            nc.scalar.activation(o_t[:, ds(i * 4 + (first_head // 2 + 2 * pp + pair), 1), 0, :]
                                                 .rearrange("p a t -> p (a t)"),
                                                 o_bank[pair][:, 0:T], ACT.Copy).then_inc(o_hi, 1)

                        refill(i, 16, base, range(8 * pp + 2, 8 * pp + 5), SLIM)
                        take_pt(0)
                        refill(i, 16, base, range(8 * pp + 5, 8 * pp + 6), SLIM)
                        take_pt(1)
                        refill(i, 16, base, range(8 * pp + 6, 8 * pp + 7), SLIM)
                        act.wait_ge(pv_done, i * 8 + (first_head + 4 * pp + 1))
                        take_pt(2)
                        act.wait_ge(pv_done, i * 8 + (first_head + 4 * pp + 2))
                        take_pt(3)
                        take_o(0)
                        refill(i, 16, base, range(8 * pp + 7, 8 * pp + 8), SLIM)
                        take_o(1)
                        wait_apart(unit_used, i * 16 + (base + 8 * pp + 8))
                        for c in range(4):
                            dst = gate_sig[:, c, :] if name == "gr" else \
                                g_attn[:, ds(i * 8 + (4 * pp + c), 1), :].rearrange("p a t -> p (a t)")
                            done = nc.scalar.activation(dst, acc_of(name, pp)[c // 2][:, c % 2 * T:c % 2 * T + T], ACT.Sigmoid,
                                                        bias=param(col, i, 8, 4 * pp + c))
                        done.then_inc(acc_free, 1)

            with act.Fori(0, 2) as i:
                for pp in range(2):
                    refill(i, 16, UNITS["attn"], range(8 * pp, 8 * pp + 8), SLIM)
                    wait_apart(mix_sum, i * 2 + (pp + 1))
                    nc.scalar.activation(act_t[:, ds(i * 8 + 4 * pp, 4), 0, :], mix_raw[:, :, :], ACT.Copy).then_inc(mix_hi, 1)
            refill(0, 0, UNITS["out"], range(28), SLIM)

            def deviation(t, count):
                act.wait_ge(ln_step, LN_STEPS * (count - 1) + LN_VAR)
                nc.scalar.activation(lnv[:, t, 2:3], lnv[:, t, 1:2], ACT.Sqrt).then_inc(ln_root, 1)

            deviation(0, 1)
            refill(0, 0, UNITS["out"], range(28, 29), SLIM)
            deviation(1, 2)
            for m in range(KT // 2):
                act.wait_ge(ln_turned, m + 1)
                for k in range(2):
                    kt = 2 * m + k
                    done = nc.scalar.activation(ln_t[:, kt, :], bank[LN_BANK[m]][:, k * T:k * T + T], ACT.Identity,
                                                scale=par[:, PAR_G1 + kt:PAR_G1 + kt + 1], bias=par[:, PAR_B1 + kt:PAR_B1 + kt + 1])
                done.then_inc(ln_made, 1)
                act.wait_ge(ln_made, m + 1)
                nc.scalar.activation(act_t[:, 2 * m:2 * m + 2, 0, :], ln_t[:, 2 * m:2 * m + 2, :], ACT.Copy).then_inc(ln_hi, 1)
                refill(0, 0, UNITS["out"], LN_REFILLS[m], SLIM)
            for half in range(2):
                with act.Fori(0, 6) as i:
                    base = UNITS[f"ff{half}"]
                    refill(i, 16, base, range(2, 12), SLIM)
                    act.wait_ge(acc_free, i * 2 + (PANELS[f"ff{half}"] + 3))
                    nc.scalar.activation(gate_c[:, :, :], gate_c[:, :, :], ACT.Gelu_apprx_tanh).then_inc(ff_gelu, 1)
                    refill(i, 16, base, range(12, 16), SLIM)
                    wait_apart(acc_free, i * 2 + (PANELS[f"ff{half}"] + 4))
                    nc.scalar.activation(f_t[:, ds(i * 4, 4), 0, :], f_raw[:, :, :], ACT.Copy).then_inc(ff_hi, 1)
                    refill(i, 16, base, range(16, 18), SLIM)
                if half == 0:
                    with act.Fori(0, 2) as i:
                        refill(i, 24, UNITS["down0"], range(2, 26), SLIM)
                else:
                    refill(0, 0, UNITS["down1"], range(2, 44), SLIM)
            for t, pieces in enumerate((POOL_PIECES[:2], POOL_PIECES[2:])):
                deviation(t, 3 + t)
                act.wait_ge(ln_step, LN_STEPS * (3 + t))
                for _, c in pieces:
                    part = res[:, t, c * D // 4:(c + 1) * D // 4]
                    nc.scalar.activation(part, part, ACT.Identity, scale=lnv[:, t, 3:4], bias=lnv[:, t, 4:5]).then_inc(ln2_norm, 1)

        @block.vector
        def _(dve):
            dve.sem_inc(acc_free, 2)
            dve.sem_inc(o_lo, 2)
            for kt in range(0, KT, 2):
                dve.wait_ge(x_hi_made, kt // 2 + 1)
                nc.vector.tensor_tensor(act_t[:, kt:kt + 2, 1, :], bank[kt // 2][:, :].rearrange("p (k t) -> p k t", k=2),
                                        act_t[:, kt:kt + 2, 0, :].bitcast(F32), ALU.subtract).then_inc(x_lo_made, 1)
            for j in range(4):
                split_lo(dve, 0, j, WIDE)

            def refill(i, stride, base, js, size):
                for j in js:
                    split_lo(dve, i * stride + base, j + 4, size)

            refill(0, 0, 0, range(3), WIDE)
            dve.wait_ge(par_turned, 1)
            nc.vector.tensor_copy(par[:, :], bank[7][:, 0:PAR_COLS]).then_inc(par_made, 1)
            dve.wait_ge(par_made, 1)

            steps = [0]

            def step(ins):
                ins.then_inc(coef_step, 1)
                steps[0] += 1
                dve.wait_ge(coef_step, steps[0])

            lam = par[:, PAR_LAM:PAR_LAM + RT]
            neg, mag, e, s, s2, poly, low = (coef[:, n, :] for n in range(7))
            step(nc.vector.tensor_scalar(neg, lam, -1.0, None, ALU.mult))
            step(nc.vector.tensor_tensor(mag, neg, lam, ALU.max))
            step(nc.vector.tensor_scalar(low, neg, 0.0, None, ALU.max))
            dve.wait_ge(coef_exp, 1)
            step(nc.vector.tensor_scalar(s2, e, 2.0, None, ALU.add))
            step(nc.vector.reciprocal(s2, s2))
            step(nc.vector.tensor_tensor(s, e, s2, ALU.mult))
            step(nc.vector.tensor_tensor(s2, s, s, ALU.mult))
            step(nc.vector.tensor_scalar(poly, s2, 1.0 / 17, None, ALU.mult))
            for n in (15, 13, 11, 9, 7, 5, 3):
                step(nc.vector.scalar_tensor_tensor(poly, poly, 1.0 / n, s2, ALU.add, ALU.mult))
            step(nc.vector.scalar_tensor_tensor(poly, poly, 1.0, s, ALU.add, ALU.mult))
            step(nc.vector.scalar_tensor_tensor(poly, poly, 2.0, low, ALU.mult, ALU.add))
            step(nc.vector.tensor_scalar(coef[:, 7, :], poly, LRU_C, None, ALU.mult))
            step(nc.vector.tensor_scalar(coef[:, 8, :], poly, -LRU_C, None, ALU.mult))

            def column(i, stride, col):
                return par[:, ds(i * stride + col, 1)]

            def recurrence(i, last_size):
                def group(part):
                    return g_work[:, ds(i * GRP, GRP), part, :]

                refill(i, 16, 0, range(3, 5), WIDE)
                for m in range(2):
                    dve.wait_ge(lru_w_hi_made, i * 2 + (m + 1))
                    nc.vector.tensor_tensor(lru_w_lo[:, m, :], lru_w[:, m, :], lru_w_hi[:, m, :].bitcast(F32), ALU.subtract)\
                        .then_inc(lru_w_lo_made, 1)
                    refill(i, 16, 0, range(5 + m, 6 + m), WIDE)
                refill(i, 16, 0, range(7, 8), WIDE)
                dve.wait_ge(unit_used, i * 16 + 8)
                for k in range(4):
                    if k:
                        dve.wait_ge(conv_step, i * 19 + 5 * k)
                    for c in range(GRP):
                        src = ACC[0][c // 2][:, c % 2 * T:c % 2 * T + T - k]
                        tap = column(i, GRP, PAR_CW + RT * (3 - k) + c)
                        if k == 0:
                            done = nc.vector.tensor_scalar(xc[:, c, :], src, tap, column(i, GRP, PAR_CB + c), ALU.mult, ALU.add)
                        else:
                            done = nc.vector.scalar_tensor_tensor(xc[:, c, k:T], src, tap, xc[:, c, k:T], ALU.mult, ALU.add)
                        done.then_inc(acc_free if k == 3 and c == GRP - 1 else conv_step, 1)
                    if k % 2:
                        refill(i, 16, 0, range(8 + k // 2, 9 + k // 2), WIDE)
                dve.wait_ge(xc_hi_made, i + 1)
                nc.vector.tensor_tensor(xc_lo[:, :, :], xc[:, :, :], xc_hi[:, :, :].bitcast(F32), ALU.subtract)\
                    .then_inc(xc_lo_made, 1)
                refill(i, 16, 0, range(10, 12), WIDE)
                refill(i, 16, 0, range(12, 15), last_size)
                dve.wait_ge(gates_read, i * GRP + (GRP + 1))
                nc.vector.tensor_tensor(lru_i[:, :, :], lru_i[:, :, :], xc[:, :, :], ALU.mult).then_inc(lru_step, 1)
                dve.wait_ge(a_made, i * GRP + GRP)
                nc.vector.tensor_tensor(group(0), lru_a[:, :, :], lru_a[:, :, :], ALU.mult).then_inc(lru_step, 1)
                dve.wait_ge(th_made, i * GRP + GRP)
                dve.wait_ge(lru_step, i * 3 + 2)
                nc.vector.scalar_tensor_tensor(group(0), group(0), 1.0, lru_r[:, :, :], ALU.add, ALU.mult).then_inc(v_made, 1)
                refill(i, 16, 0, range(15, 16), last_size)
                dve.wait_ge(root_made, i + 1)
                nc.vector.scalar_tensor_tensor(lru_i[:, :, :], group(0), 2.0 ** -32, lru_i[:, :, :], ALU.mult, ALU.mult)\
                    .then_inc(lru_step, 1)
                dve.wait_ge(lru_step, i * 3 + 3)
                for c in range(GRP):
                    nc.vector.tensor_tensor_scan(xc[:, c, :], lru_a[:, c, :], lru_i[:, c, :], 0.0, ALU.mult, ALU.add)\
                        .then_inc(h_made, 1)
                refill(i, 16, 0, range(16, 18), last_size)
                dve.wait_ge(acc_free, i * 2 + 4)
                dve.wait_ge(h_made, i * GRP + GRP)
                nc.vector.tensor_tensor(xc[:, :, :], xc[:, :, :], group(1), ALU.mult).then_inc(g_prod, 1)
                refill(i, 16, 0, range(18, 19), last_size)
                dve.wait_ge(g_hi, i + 1)
                nc.vector.tensor_tensor(g_t[:, ds(i * GRP, GRP), 1, :], xc[:, :, :],
                                        g_t[:, ds(i * GRP, GRP), 0, :].bitcast(F32), ALU.subtract).then_inc(g_lo, 1)

            with dve.Fori(0, 3) as i:
                recurrence(i, WIDE)
            recurrence(3, SLIM)

            with dve.Fori(0, 2) as i:
                refill(i, 16, UNITS["q"], range(3, 19), SLIM)
            refill(0, 0, UNITS["kv"], range(3, 4), SLIM)
            refill(0, 0, UNITS["kv"], range(4, 8), WIDE)
            refill(0, 0, UNITS["rnn"], range(28), WIDE)
            refill(0, 0, UNITS["rnn"], range(28, 32), SLIM)

            bias, sink_part, sums = ssmall[:, 0, :], ssmall[:, 1, :], ssmall[:, 2, :]
            denom, top = ssmall[:, 3, :], ssmall[:, 4, :]

            def by_block(tile, blk):
                return tile.rearrange("p (h b) -> p h b", b=2)[:, :, blk]

            SOFT = 7
            for name, first_head in (("gr", 0), ("ga", 16)):
                with dve.Fori(0, 2) as i:
                    for pp in range(2):
                        base = UNITS[name]

                        def soft(n):
                            dve.wait_ge(soft_step, i * (2 * SOFT) + (SOFT * (first_head // 4 + pp) + n))

                        sink = sinks[:, ds(i * 8 + (first_head + 4 * pp), 4)]
                        refill(i, 16, base, range(8 * pp, 8 * pp + 1), SLIM)
                        dve.wait_ge(dist_loaded, 16)
                        for hh in range(4):
                            dve.wait_ge(scores_done, i * 8 + (first_head + 4 * pp + hh + 1))
                            nc.vector.scalar_tensor_tensor(
                                s_buf[:, hh, :], dist, const[:, ds(i * 8 + (CONST_SLOPE + first_head + 4 * pp + hh), 1)],
                                s_bank[hh][:, 0:3 * P], ALU.mult, ALU.add).then_inc(scores_taken, 1)
                        dve.wait_ge(scores_taken, i * 8 + (first_head + 4 * pp + 4))
                        nc.vector.tensor_reduce(smax[:, :, :], s_buf[:, :, :].rearrange("p h (s k) -> p h s k", s=3), AX.X, ALU.max)\
                            .then_inc(soft_step, 1)
                        soft(1)
                        nc.vector.scalar_tensor_tensor(by_block(top, 0), sink, 1.0 / SCALE, smax[:, :, 0], ALU.mult, ALU.max)\
                            .then_inc(soft_step, 1)
                        nc.vector.scalar_tensor_tensor(by_block(top, 1), sink, 1.0 / SCALE, smax[:, :, 2], ALU.mult, ALU.max)\
                            .then_inc(soft_step, 1)
                        soft(3)
                        nc.vector.tensor_tensor(by_block(top, 0), by_block(top, 0), smax[:, :, 1], ALU.max).then_inc(soft_step, 1)
                        soft(4)
                        nc.vector.tensor_scalar(bias, top, -SCALE, None, ALU.mult).then_inc(soft_step, 1)
                        soft(5)
                        for blk in range(2):
                            nc.vector.tensor_tensor(by_block(sink_part, blk), by_block(bias, blk), sink, ALU.add)\
                                .then_inc(bias_made if blk else soft_step, 1)
                        refill(i, 16, base, range(8 * pp + 1, 8 * pp + 2), SLIM)
                        dve.wait_ge(exp_made, i * 2 + (first_head // 4 + pp + 1))
                        nc.vector.tensor_tensor(denom, sums, sink_part, ALU.add).then_inc(soft_step, 1)
                        soft(7)
                        nc.vector.reciprocal(denom, denom).then_inc(merged, 1)
                        dve.wait_ge(merged, i * MERGED[name][1] + (MERGED[name][0] + MERGED[name][1] // 2 * pp + 1))
                        for hh in range(4):
                            nc.vector.tensor_scalar(s_buf[:, hh, 0:T], s_buf[:, hh, 0:T], denom[:, 2 * hh:2 * hh + 1], None, ALU.mult)
                            nc.vector.tensor_scalar(s_buf[:, hh, T:3 * P], s_buf[:, hh, T:3 * P], denom[:, 2 * hh + 1:2 * hh + 2], None,
                                                    ALU.mult).then_inc(probs_made, 1)

                        def take_o(pair):
                            dve.wait_ge(o_hi, i * 4 + (first_head // 2 + 2 * pp + pair + 1))
                            tile = i * 4 + (first_head // 2 + 2 * pp + pair)
                            nc.vector.tensor_tensor(o_t[:, ds(tile, 1), 1, :].rearrange("p a t -> p (a t)"),
                                                    o_bank[pair][:, 0:T],
                                                    o_t[:, ds(tile, 1), 0, :].rearrange("p a t -> p (a t)").bitcast(F32),
                                                    ALU.subtract).then_inc(o_lo, 1)

                        refill(i, 16, base, range(8 * pp + 2, 8 * pp + 7), SLIM)
                        take_o(0)
                        refill(i, 16, base, range(8 * pp + 7, 8 * pp + 8), SLIM)
                        take_o(1)
                        if name == "gr":
                            dve.wait_ge(acc_free, i * 2 + (PANELS[name] + pp + 3))
                            nc.vector.tensor_tensor(merge[:, ds(i * 8 + 4 * pp, 4), :], merge[:, ds(i * 8 + 4 * pp, 4), :],
                                                    gate_sig, ALU.mult).then_inc(merged, 1)

            with dve.Fori(0, 2) as i:
                for pp in range(2):
                    refill(i, 16, UNITS["attn"], range(8 * pp, 8 * pp + 8), SLIM)
                    dve.wait_ge(unit_used, i * 16 + (UNITS["attn"] + 8 * pp + 8))
                    for b in range(2):
                        nc.vector.tensor_tensor(mix_raw[:, 2 * b:2 * b + 2, :],
                                                acc_of("attn", pp)[b][:, :].rearrange("p (k t) -> p k t", k=2),
                                                g_attn[:, ds(i * 8 + (4 * pp + 2 * b), 2), :], ALU.mult)\
                            .then_inc(acc_free if b else attn_gated, 1)
                    dve.wait_ge(attn_gated, i * 2 + (pp + 1))
                    dve.wait_ge(acc_free, i * 2 + (PANELS["attn"] + pp + 3))
                    nc.vector.tensor_tensor(mix_raw[:, :, :], mix_raw[:, :, :], merge[:, ds(i * 8 + 4 * pp, 4), :], ALU.add)\
                        .then_inc(mix_sum, 1)
                    dve.wait_ge(mix_hi, i * 2 + (pp + 1))
                    nc.vector.tensor_tensor(act_t[:, ds(i * 8 + 4 * pp, 4), 1, :], mix_raw[:, :, :],
                                            act_t[:, ds(i * 8 + 4 * pp, 4), 0, :].bitcast(F32), ALU.subtract).then_inc(mix_lo, 1)

            def add_residual(i, name, pp, n_units, scale):
                dve.wait_ge(unit_used, i * (2 * n_units) + (UNITS[name] + n_units * (pp + 1)))
                for t in range(TOK):
                    part = res[:, t, ds(i * 1024 + 512 * pp, 512)]
                    nc.vector.scalar_tensor_tensor(part, part, scale, acc_of(name, pp)[t][:, :], ALU.mult, ALU.add)\
                        .then_inc(acc_free if t else res_step, 1)

            def panel_stats(i, name, pp, step0):
                dve.wait_ge(res_step, i * 2 + (step0 + pp + 1))
                dve.wait_ge(acc_free, i * 2 + (PANELS[name] + pp + 3))
                for t in range(TOK):
                    nc.vector.bn_stats(stats[:, t, ds(i * 2 + pp, 1), :].rearrange("p a s -> p (a s)"),
                                       res[:, t, ds(i * 1024 + 512 * pp, 512)]).then_inc(stat_step, 1)

            def last_sums(name, t, scale, count):
                if t == 0:
                    dve.wait_ge(tile0_summed, (count + 1) // 2)
                else:
                    dve.wait_ge(unit_used, UNITS["ff0"] if name == "out" else LAST_UNIT)
                part = res[:, t, 3 * D // 4:]
                nc.vector.scalar_tensor_tensor(part, part, scale, acc_of(name, 3)[t][:, :], ALU.mult, ALU.add)\
                    .then_inc(acc_free if t else res_step, 1)
                if t == 0:
                    dve.wait_ge(res_step, 4 if name == "out" else 12)
                else:
                    dve.wait_ge(acc_free, PANELS[name] + 6)
                nc.vector.bn_stats(stats[:, t, 3, :], part).then_inc(stat_step, 1)
                dve.wait_ge(stat_step, 7 + t if name == "out" else 15 + t)
                before = LN_STEPS * (count - 1)
                nc.vector.bn_aggr(lnv[:, t, 0:2], stats[:, t, :, :].rearrange("p a s -> p (a s)")).then_inc(ln_step, 1)
                dve.wait_ge(ln_step, before + 1)
                nc.vector.tensor_scalar(lnv[:, t, 1:2], lnv[:, t, 1:2], LN_EPS, None, ALU.add).then_inc(ln_step, 1)
                dve.wait_ge(ln_root, count)
                nc.vector.reciprocal(lnv[:, t, 3:4], lnv[:, t, 2:3]).then_inc(ln_step, 1)
                dve.wait_ge(ln_step, before + 3)
                nc.vector.scalar_tensor_tensor(lnv[:, t, 4:5], lnv[:, t, 0:1], -1.0, lnv[:, t, 3:4], ALU.mult, ALU.mult)\
                    .then_inc(ln_step, 1)

            for pp in range(3):
                refill(0, 0, UNITS["out"], range(8 * pp, 8 * pp + 8), SLIM)
                dve.wait_ge(res_loaded, 32)
                add_residual(0, "out", pp, 8, ALPHA)
                panel_stats(0, "out", pp, 0)
            refill(0, 0, UNITS["out"], range(24, 28), SLIM)
            for t in range(TOK):
                last_sums("out", t, ALPHA, t + 1)
                for c in range(4):
                    part = res[:, t, c * D // 4:(c + 1) * D // 4]
                    nc.vector.tensor_scalar(part, part, lnv[:, t, 0:1], lnv[:, t, 3:4], ALU.subtract, ALU.mult).then_inc(ln_norm, 1)
                if t == 0:
                    refill(0, 0, UNITS["out"], range(28, 29), SLIM)
            for m in range(KT // 2):
                dve.wait_ge(ln_hi, m + 1)
                nc.vector.tensor_tensor(act_t[:, 2 * m:2 * m + 2, 1, :], ln_t[:, 2 * m:2 * m + 2, :],
                                        act_t[:, 2 * m:2 * m + 2, 0, :].bitcast(F32), ALU.subtract).then_inc(ln_lo, 1)
                refill(0, 0, UNITS["out"], LN_REFILLS[m], SLIM)

            for half in range(2):
                name = f"ff{half}"
                with dve.Fori(0, 6) as i:
                    base = UNITS[name]
                    refill(i, 16, base, range(2, 8), SLIM)
                    dve.wait_ge(unit_used, i * 16 + (base + 8))
                    for k in range(3):
                        if k:
                            dve.wait_ge(ff_conv, i * 11 + (66 * half + 4 * k))
                        for c in range(4):
                            src = acc_of(name, 0)[c // 2][:, c % 2 * T:c % 2 * T + T - k]
                            tap = column(i, 4, PAR_FW + 2 * FT_HALF * (2 - k) + FT_HALF * half + c)
                            if k == 0:
                                done = nc.vector.tensor_scalar(gate_c[:, c, :], src, tap,
                                                               column(i, 4, PAR_FB + FT_HALF * half + c), ALU.mult, ALU.add)
                            else:
                                done = nc.vector.scalar_tensor_tensor(gate_c[:, c, k:T], src, tap, gate_c[:, c, k:T], ALU.mult, ALU.add)
                            done.then_inc(acc_free if k == 2 and c == 3 else ff_conv, 1)
                    refill(i, 16, base, range(8, 16), SLIM)
                    dve.wait_ge(unit_used, i * 16 + (base + 16))
                    dve.wait_ge(ff_gelu, i + (6 * half + 1))
                    for b in range(2):
                        nc.vector.tensor_tensor(f_raw[:, 2 * b:2 * b + 2, :], acc_of(name, 1)[b][:, :].rearrange("p (k t) -> p k t", k=2),
                                                gate_c[:, 2 * b:2 * b + 2, :], ALU.mult).then_inc(acc_free if b else ff_prod, 1)
                    dve.wait_ge(ff_hi, i + (6 * half + 1))
                    nc.vector.tensor_tensor(f_t[:, ds(i * 4, 4), 1, :], f_raw[:, :, :],
                                            f_t[:, ds(i * 4, 4), 0, :].bitcast(F32), ALU.subtract).then_inc(ff_lo, 1)
                    refill(i, 16, base, range(16, 18), SLIM)
                name = f"down{half}"
                if half == 0:
                    dve.wait_ge(res_made, 2 * TOK)
                    with dve.Fori(0, 2) as i:
                        for pp in range(2):
                            refill(i, 24, UNITS[name], range(12 if pp else 2, 12 * pp + 12), SLIM)
                            add_residual(i, name, pp, 12, ALPHA)
                        refill(i, 24, UNITS[name], range(24, 26), SLIM)
                else:
                    for pp in range(3):
                        refill(0, 0, UNITS[name], range(12 * pp if pp else 2, 12 * pp + 12), SLIM)
                        add_residual(0, name, pp, 12, 1.0)
                        panel_stats(0, name, pp, 8)
                    refill(0, 0, UNITS[name], range(36, 44), SLIM)
            dve.wait_ge(ln_loaded, 64)
            n = 0
            for t, pieces in enumerate((DVE_PIECES[:2], DVE_PIECES[2:])):
                last_sums("down1", t, 1.0, 3 + t)
                for _, c in pieces:
                    cols = slice(c * D // 4, (c + 1) * D // 4)
                    part = res[:, t, cols]
                    nc.vector.scalar_tensor_tensor(part, part, lnv[:, t, 0:1], ln_gb[:, 0, cols], ALU.subtract, ALU.mult)\
                        .then_inc(ln2_step, 1)
                    n += 1
                    dve.wait_ge(ln2_step, n)
                    nc.vector.scalar_tensor_tensor(part, part, lnv[:, t, 3:4], ln_gb[:, 1, cols], ALU.mult, ALU.add)\
                        .then_inc(ln2_done[0], 1)


LN_STEPS = 4
LN_VAR = 2
LN_BANK = [3, 4, 0, 2, 5, 6, 7, 1]
LN_REFILLS = [(29,), (30,), (31,), (32,), (33,), (), (), ()]
DVE_PIECES = [(0, 0), (0, 1), (1, 1), (1, 2), (1, 3)]
POOL_PIECES = [(0, 2), (0, 3), (1, 0)]
OUT_PIECES = [(0, 0, D // 2, 0, 2), (0, D // 2, D, 1, 2), (1, D // 4, 3 * D // 4, 0, 4), (1, 0, D // 4, 1, 3),
              (1, 3 * D // 4, D, 0, 5)]
MERGED = {"gr": (0, 4), "ga": (8, 2)}


_INS = ["x", "w_in", "b_gate", "rnn_conv_w", "rnn_conv_b", "lru_wa", "lru_ba", "lru_wi", "lru_bi",
        "lru_lambda", "attn_sinks", "w_attn_proj", "w_rnn_proj", "w_out", "ln1_g", "ln1_b", "ffn_w_up",
        "ffn_w_gate", "ffn_conv_w", "ffn_conv_b", "ffn_w_down", "ln2_g", "ln2_b"]


def shape_constants():
    import numpy as np

    q = np.arange(P)[:, None]
    k = np.arange(2 * P)[None, :]
    d = P + q - k
    neg = np.where((d >= 0) & (d < P), -d, -1e30).astype(np.float32)
    slopes = (2.0 ** (-8.0 * np.arange(1, NH + 1) / NH) / SCALE).astype(np.float32)
    return np.ascontiguousarray(np.concatenate(
        [np.eye(P, dtype=np.float32), np.broadcast_to(slopes, (P, NH)), neg, neg[:, P:]], axis=1))


def kernel(**inputs):
    import numpy as _np
    import concourse.bacc as _bacc
    from concourse import mybir as _mybir
    from concourse.bass_utils import run_bass_kernel_spmd as _run

    nc = _bacc.Bacc("TRN2", target_bir_lowering=False, num_devices=1)
    arrays = {"in_consts_dram": shape_constants()}
    for name in _INS:
        arrays[f"in_{name}_dram"] = _np.ascontiguousarray(inputs[name])
    args = [nc.dram_tensor(n, a.shape, _mybir.dt.from_np(a.dtype), kind="ExternalInput").ap() for n, a in arrays.items()]
    args.append(nc.dram_tensor("out_0_dram", (1, T, D), _mybir.dt.float32, kind="ExternalOutput").ap())
    layer_kernel(nc, *args)
    r = _run(nc, [arrays], core_ids=[0])
    return r.results[0]["out_0_dram"]
```
